# Optimizing a Trainium2 kernel written in Bass

```python
import jax, jax.numpy as jnp
from jax import lax
import numpy as np

D_MODEL = 1024
BATCH = 1
SEQ = 256
DEPTH = 4

N_MIXERS = 3
N_A = (DEPTH + 2) // 3
N_B = (DEPTH + 1) // 3
N_C = DEPTH // 3
SC_WIDTH = 3
ATTN_HEADS = 16
ATTN_KV_HEADS = 4
HEAD_DIM = 64
WINDOW = 128
BLOCK = 128
CONF_WIDTH = 31
MEM_LEN = 256
XATTN_HEADS = 4
XATTN_HEAD_DIM = D_MODEL // XATTN_HEADS
D_FF = 2816
FFN_CONV_WIDTH = 3
EPS = 1e-6

kernel_name = "hybrid_shortconv_swa_conformer_trunk"

def rmsnorm(x, g):
    x32 = x.astype(jnp.float32)
    y = x32 * lax.rsqrt(jnp.mean(x32 * x32, axis=-1, keepdims=True) + EPS)
    return y.astype(x.dtype) * g

def layernorm(x, g, b):
    x32 = x.astype(jnp.float32)
    mu = jnp.mean(x32, axis=-1, keepdims=True)
    xc = x32 - mu
    y = xc * lax.rsqrt(jnp.mean(xc * xc, axis=-1, keepdims=True) + EPS)
    return y.astype(x.dtype) * g + b

def causal_dwconv(x, w):
    K, C = w.shape
    return lax.conv_general_dilated(
        x, w[:, None, :], window_strides=(1,), padding=[(K - 1, 0)],
        dimension_numbers=('NWC', 'WIO', 'NWC'), feature_group_count=C)

def alibi_slopes(n_heads):
    return 2.0 ** (-8.0 * jnp.arange(1, n_heads + 1, dtype=jnp.float32) / n_heads)

def short_conv_mixer(h, w_in, conv_w, w_out):
    b_gate, c_gate, v = jnp.split(h @ w_in, 3, axis=-1)
    return (b_gate * causal_dwconv(c_gate * v, conv_w)) @ w_out

def swa_sink_attention(h, w_qkv, b_qkv, sinks, w_o, b_o):
    bsz, s_len, _ = h.shape
    G = ATTN_HEADS // ATTN_KV_HEADS
    NB = s_len // BLOCK
    qkv = h @ w_qkv + b_qkv
    q, k, v = jnp.split(qkv, [ATTN_HEADS * HEAD_DIM, (ATTN_HEADS + ATTN_KV_HEADS) * HEAD_DIM], axis=-1)
    q = q.reshape(bsz, NB, BLOCK, ATTN_KV_HEADS, G, HEAD_DIM)

    def band(t):
        t = jnp.pad(t, ((0, 0), (BLOCK, 0), (0, 0))).reshape(bsz, NB + 1, BLOCK, ATTN_KV_HEADS, HEAD_DIM)
        return jnp.concatenate([t[:, :-1], t[:, 1:]], axis=2)

    kb, vb = band(k), band(v)
    s = jnp.einsum('bnqkgd,bnskd->bnkgqs', q, kb, preferred_element_type=jnp.float32) * (HEAD_DIM ** -0.5)
    dist = BLOCK + jnp.arange(BLOCK)[:, None] - jnp.arange(2 * BLOCK)[None, :]
    key_pos = jnp.arange(NB)[:, None] * BLOCK - BLOCK + jnp.arange(2 * BLOCK)[None, :]
    valid = ((dist >= 0) & (dist < WINDOW))[None] & (key_pos >= 0)[:, None, :]
    slopes = alibi_slopes(ATTN_HEADS).reshape(ATTN_KV_HEADS, G)
    s = s - slopes[:, :, None, None] * dist.astype(jnp.float32)
    s = jnp.where(valid[None, :, None, None], s, -jnp.inf)
    sink = sinks.astype(jnp.float32).reshape(ATTN_KV_HEADS, G)[None, None, :, :, None]
    m = jnp.maximum(s.max(axis=-1), sink)
    p = jnp.exp(s - m[..., None])
    p = p / (p.sum(axis=-1) + jnp.exp(sink - m))[..., None]
    o = jnp.einsum('bnkgqs,bnskd->bnqkgd', p.astype(vb.dtype), vb)
    return o.reshape(bsz, s_len, ATTN_HEADS * HEAD_DIM) @ w_o + b_o

def conformer_conv_module(h, w_pw1, b_pw1, w_dw, b_dw, ln_g, ln_b, w_pw2, b_pw2):
    a, gate = jnp.split(h @ w_pw1 + b_pw1, 2, axis=-1)
    u = a * jax.nn.sigmoid(gate)
    u = causal_dwconv(u, w_dw) + b_dw
    u = layernorm(u, ln_g, ln_b)
    return jax.nn.silu(u) @ w_pw2 + b_pw2

def memory_cross_attention(h, mem, g_mem, w_q, w_kv, w_o):
    bsz, s_len, _ = h.shape
    q = (h @ w_q).reshape(bsz, s_len, XATTN_HEADS, XATTN_HEAD_DIM)
    k, v = jnp.split(rmsnorm(mem, g_mem) @ w_kv, 2, axis=-1)
    k = k.reshape(bsz, -1, XATTN_HEADS, XATTN_HEAD_DIM)
    v = v.reshape(bsz, -1, XATTN_HEADS, XATTN_HEAD_DIM)
    s = jnp.einsum('bshd,bmhd->bhsm', q, k, preferred_element_type=jnp.float32) * (XATTN_HEAD_DIM ** -0.5)
    p = jax.nn.softmax(s, axis=-1)
    o = jnp.einsum('bhsm,bmhd->bshd', p.astype(v.dtype), v).reshape(bsz, s_len, D_MODEL)
    return o @ w_o

def conv_gated_mlp(h, w_up, conv_w, w_down):
    gate, up = jnp.split(h @ w_up, 2, axis=-1)
    return (jax.nn.silu(causal_dwconv(gate, conv_w)) * up) @ w_down

def setup_inputs(seed: int = 0) -> dict:
    key = jax.random.key(seed)
    ks = iter(jax.random.split(key, 40))
    D = D_MODEL
    QKV = (ATTN_HEADS + 2 * ATTN_KV_HEADS) * HEAD_DIM

    def nrm(shape, scale):
        return jax.random.normal(next(ks), shape, jnp.float32) * scale

    def gain(shape):
        return 1.0 + nrm(shape, 0.02)

    return {
        "x": nrm((BATCH, SEQ, D), 1.0),
        "mem": nrm((BATCH, MEM_LEN, D), 1.0),
        "norm_mix": gain((DEPTH, D)),
        "norm_xattn": gain((DEPTH, D)),
        "norm_mem": gain((DEPTH, D)),
        "norm_ffn": gain((DEPTH, D)),
        "norm_final": gain((D,)),
        "a_w_in": nrm((N_A, D, 3 * D), D ** -0.5),
        "a_conv": nrm((N_A, SC_WIDTH, D), SC_WIDTH ** -0.5),
        "a_w_out": nrm((N_A, D, D), D ** -0.5),
        "b_w_qkv": nrm((N_B, D, QKV), D ** -0.5),
        "b_b_qkv": nrm((N_B, QKV), 0.02),
        "b_sinks": nrm((N_B, ATTN_HEADS), 0.5),
        "b_w_o": nrm((N_B, ATTN_HEADS * HEAD_DIM, D), (ATTN_HEADS * HEAD_DIM) ** -0.5),
        "b_b_o": nrm((N_B, D), 0.02),
        "c_w_pw1": nrm((N_C, D, 2 * D), D ** -0.5),
        "c_b_pw1": nrm((N_C, 2 * D), 0.02),
        "c_w_dw": nrm((N_C, CONF_WIDTH, D), CONF_WIDTH ** -0.5),
        "c_b_dw": nrm((N_C, D), 0.02),
        "c_ln_g": gain((N_C, D)),
        "c_ln_b": nrm((N_C, D), 0.02),
        "c_w_pw2": nrm((N_C, D, D), D ** -0.5),
        "c_b_pw2": nrm((N_C, D), 0.02),
        "x_w_q": nrm((DEPTH, D, D), D ** -0.5),
        "x_w_kv": nrm((DEPTH, D, 2 * D), D ** -0.5),
        "x_w_o": nrm((DEPTH, D, D), D ** -0.5),
        "f_w_up": nrm((DEPTH, D, 2 * D_FF), D ** -0.5),
        "f_conv": nrm((DEPTH, FFN_CONV_WIDTH, D_FF), FFN_CONV_WIDTH ** -0.5),
        "f_w_down": nrm((DEPTH, D_FF, D), D_FF ** -0.5),
    }

def reference(x, mem, norm_mix, norm_xattn, norm_mem, norm_ffn, norm_final,
              a_w_in, a_conv, a_w_out,
              b_w_qkv, b_b_qkv, b_sinks, b_w_o, b_b_o,
              c_w_pw1, c_b_pw1, c_w_dw, c_b_dw, c_ln_g, c_ln_b, c_w_pw2, c_b_pw2,
              x_w_q, x_w_kv, x_w_o,
              f_w_up, f_conv, f_w_down):
    for i in range(DEPTH):
        kind, j = i % N_MIXERS, i // N_MIXERS
        h = rmsnorm(x, norm_mix[i])
        if kind == 0:
            y = short_conv_mixer(h, a_w_in[j], a_conv[j], a_w_out[j])
        elif kind == 1:
            y = swa_sink_attention(h, b_w_qkv[j], b_b_qkv[j], b_sinks[j], b_w_o[j], b_b_o[j])
        else:
            y = conformer_conv_module(h, c_w_pw1[j], c_b_pw1[j], c_w_dw[j], c_b_dw[j],
                                      c_ln_g[j], c_ln_b[j], c_w_pw2[j], c_b_pw2[j])
        x = x + y
        x = x + memory_cross_attention(rmsnorm(x, norm_xattn[i]), mem, norm_mem[i],
                                       x_w_q[i], x_w_kv[i], x_w_o[i])
        x = x + conv_gated_mlp(rmsnorm(x, norm_ffn[i]), f_w_up[i], f_conv[i], f_w_down[i])
    return rmsnorm(x, norm_final)


_drawn_inputs = setup_inputs


def setup_inputs(seed=0):
    import zlib

    import numpy as np

    out = dict(_drawn_inputs(seed))
    spreads = {}
    factors = {'norm_xattn': 8.0,
     'norm_mem': 8.0,
     'norm_final': 2.742,
     'b_b_qkv': 3.403,
     'b_b_o': 3.12,
     'c_b_pw1': 6.017,
     'c_b_dw': 2.965,
     'c_ln_g': 5.393,
     'c_ln_b': 6.791,
     'c_b_pw2': 3.874}
    for name, (base, spread) in spreads.items():
        noise = np.random.default_rng([zlib.crc32(name.encode()), seed]).standard_normal(out[name].shape)
        drawn = base * np.exp(spread * noise) if base else spread * noise
        out[name] = __import__('jax').numpy.asarray(drawn.astype(out[name].dtype))
    for name, factor in factors.items():
        out[name] = (out[name] * factor).astype(out[name].dtype)
    return out
```

```python
from contextlib import ExitStack

import concourse.bass as bass
from concourse import mybir

ALU = mybir.AluOpType
ACT = mybir.ActivationFunctionType
AX_X = mybir.AxisListType.X
F32 = mybir.dt.float32
F32R = mybir.dt.float32r

P = 128
D = 1024
T = 256
DEPTH = 4
KC = D // P
TT = T // P
FF = 2816
FC = FF // P
UC = 256
UB = UC // P
PAIRS = FF // UC
NOUT = D // UC
SLOTS = 3
AHEAD = 2
TAPS = 3
CTAPS = 31
HEADS = 16
KVH = 4
HD = 64
XH = 4
XHD = D // XH
PAD = CTAPS - 1
CPARTS = 4
CSTEP = -(-CTAPS // CPARTS)
GROUP = 4
EPS = 1e-6
FAR = 1e30




ADDS = {
    "start": dict(x=4, su=1, r=1, tr=10, tu=6, g=1, u=1),
    "mem_scale": dict(a=4, y=4),
    "memkv": dict(kv=1),
    "norm": dict(a=4, y=4, st=1, v=1, r=1),
    "sconv": dict(a=4, y=4, g=4, u=4),
    "resid": dict(x=4, su=1),
    "q": dict(q=4),
    "qkv": dict(q=6),
    "scores": dict(h=GROUP),
    "attend": dict(a=XH, y=XH, hd=GROUP),
    "swa_attend": dict(a=1, y=1, hd=GROUP),
    "pw1": dict(g=4, gl=4),
    "lnorm": dict(a=4, x=4, su=2, st=2, v=1, r=1, c=4),
    "ffn": dict(a=PAIRS, y=PAIRS, g=PAIRS, c=PAIRS, si=PAIRS),
    "down": dict(x=4, su=1, d=3),
    "final": dict(st=1, v=1, r=1, c=4, tr=4),
}


class Chain:

    def __init__(self, eng, sem):
        self.eng, self.sem, self.n, self.i, self.per = eng, sem, 0, 0, 0

    def mark(self, ins):
        self.n += 1
        ins.then_inc(self.sem, 1)
        return self.n

    def wait(self, mark):
        self.eng.wait_ge(self.sem, mark if self.per == 0 else self.i * self.per + mark)

    def link(self, ins):
        self.wait(self.mark(ins))

    def enter(self, i, per):
        self.i, self.per, self.start = i, per, self.n

    def leave(self, trips):
        assert self.n - self.start == self.per, (self.n - self.start, self.per)
        self.n = self.start + trips * self.per
        self.i = self.per = 0



def build(nc, a, out):
    params = [
        ("norm_mem", a["norm_mem"].rearrange("i (c p) -> (i c) p", p=P)),
        ("norm_mix", a["norm_mix"].rearrange("i (c p) -> (i c) p", p=P)),
        ("norm_xattn", a["norm_xattn"].rearrange("i (c p) -> (i c) p", p=P)),
        ("norm_ffn", a["norm_ffn"].rearrange("i (c p) -> (i c) p", p=P)),
        ("a_conv", a["a_conv"].rearrange("j k (c p) -> (j k c) p", p=P)),
        ("norm_final", a["norm_final"].rearrange("(c p) -> c p", p=P)),
        ("b_b_qkv", a["b_b_qkv"].rearrange("j (c p) -> (j c) p", p=P)),
        ("b_b_o", a["b_b_o"].rearrange("j (c p) -> (j c) p", p=P)),
        ("c_b_pw1", a["c_b_pw1"].rearrange("j (c p) -> (j c) p", p=P)),
        ("c_b_dw", a["c_b_dw"].rearrange("j (c p) -> (j c) p", p=P)),
        ("c_ln_g", a["c_ln_g"].rearrange("j (c p) -> (j c) p", p=P)),
        ("c_ln_b", a["c_ln_b"].rearrange("j (c p) -> (j c) p", p=P)),
        ("c_b_pw2", a["c_b_pw2"].rearrange("j (c p) -> (j c) p", p=P)),
        ("f_conv", a["f_conv"].rearrange("i k (c p) -> (i k c) p", p=P)),
        ("c_w_dw", a["c_w_dw"].rearrange("j k (c p) -> (j k c) p", p=P)),
    ]
    col, nrow = {}, 0
    for key, ap in params:
        col[key] = nrow
        nrow += ap.shape[0]
    groups = -(-nrow // P)
    pieces = []
    for key, ap in params:
        r = 0
        while r < ap.shape[0]:
            g, p0 = divmod(col[key] + r, P)
            k = min(ap.shape[0] - r, P - p0)
            pieces.append((g, p0, k, ap[r:r + k, :]))
            r += k

    stages = []
    counts = dict(n=0)

    def stage(kind, units=0, **kw):
        stages.append(dict(kind=kind, n0=counts["n"], units=units, c=dict(counts), **kw))
        counts["n"] += units
        for key, v in ADDS[kind].items():
            counts[key] = counts.get(key, 0) + v

    for adds in ADDS.values():
        for key in adds:
            counts.setdefault(key, 0)
    filled = [0]

    def fill(count):
        for _ in range(count):
            layer, k = divmod(filled[0], 2 * NOUT)
            if k == 0:
                stage("mem_scale", layer=layer)
            stage("memkv", 1, layer=layer, k=k)
            filled[0] += 1

    def shortconv(layer, j, f_norm, f_mid):
        stage("norm", g=("norm_mix", layer))
        fill(f_norm)
        stage("sconv", 3 * NOUT, j=j)
        fill(f_mid)
        stage("resid", NOUT, w=a["a_w_out"][j], bias=None)

    def xattn(layer, f_norm, f_softmax):
        stage("norm", g=("norm_xattn", layer))
        fill(f_norm)
        stage("q", NOUT, layer=layer)
        stage("scores", layer=layer, group=0)
        fill(f_softmax)
        stage("attend", layer=layer, group=0)
        stage("resid", NOUT, w=a["x_w_o"][layer], bias=None)

    def ffn(layer, f_norm, f_down):
        stage("norm", g=("norm_ffn", layer))
        fill(f_norm)
        stage("ffn", 3 * PAIRS - 1, layer=layer)
        fill(f_down)
        stage("down", 1, layer=layer)

    stage("start")
    fill(4)
    shortconv(0, 0, 0, 1)
    xattn(0, 1, 2)
    ffn(0, 1, 1)
    stage("norm", g=("norm_mix", 1))
    fill(1)
    stage("qkv", 6)
    for group in range(HEADS // GROUP):
        stage("scores", layer=None, group=group)
        fill(1)
        stage("swa_attend", layer=None, group=group)
    stage("resid", NOUT, w=a["b_w_o"][0], bias="b_b_o")
    fill(4 * NOUT - filled[0])
    xattn(1, 1, 1)
    ffn(1, 1, 1)
    stage("norm", g=("norm_mix", 2))
    fill(1)
    stage("pw1", 2 * NOUT)
    conv_fills = CPARTS * NOUT - (2 * NOUT - 1)
    part = 2 * NOUT - 1
    for _ in range(conv_fills):
        fill(1)
        stages[-1]["part"] = part
        part += 1
    stage("lnorm")
    stage("resid", NOUT, w=a["c_w_pw2"][0], bias="c_b_pw2")
    xattn(2, 0, 1)
    ffn(2, 0, 0)
    shortconv(3, 1, 8 * DEPTH - filled[0], 0)
    xattn(3, 0, 0)
    ffn(3, 0, 0)
    stage("final")
    assert filled[0] == 2 * NOUT * DEPTH
    N = counts["n"]

    with ExitStack() as ctx:
        def sb(name, shape, dt=F32):
            return ctx.enter_context(nc.sbuf_tensor(name, shape, dt))

        def ps(name, shape):
            return ctx.enter_context(nc.psum_tensor(name, shape, F32))

        def sem(name):
            return ctx.enter_context(nc.semaphore(name))

        raw = [sb(f"raw{s}", [P, KC, UC]) for s in range(SLOTS)]
        whi = [sb(f"whi{s}", [P, KC, UC], F32R) for s in range(SLOTS)]
        wlo = [sb(f"wlo{s}", [P, KC, UC], F32R) for s in range(SLOTS)]
        x = sb("x", [P, KC, T])
        h_hi, h_lo = sb("h_hi", [P, KC, T], F32R), sb("h_lo", [P, KC, T], F32R)
        m_hi, m_lo = sb("m_hi", [P, KC, T], F32R), sb("m_lo", [P, KC, T], F32R)
        z_hi, z_lo = sb("z_hi", [P, UB, T], F32R), sb("z_lo", [P, UB, T], F32R)
        memn = sb("memn", [P, KC, T])
        g_hi, g_lo = sb("g_hi", [P, KC, T], F32R), sb("g_lo", [P, KC, T], F32R)
        memk = [sb(f"memk{i}", [P, KC, T]) for i in range(2)]
        memv = [sb(f"memv{i}", [P, TT, D]) for i in range(2)]
        mid = sb("mid", [P, KC, PAD + T])
        inner = mid[:, :, PAD:PAD + T]
        pad3 = sb("pad3", [P, UB, TAPS - 1 + T])
        cv = sb("cv", [P, UB, T])
        y = [sb(f"y{i}", [P, UB, T]) for i in range(2)]
        ssum = sb("ssum", [P, UB, T])
        rs, var, nt = sb("rs", [P, T]), sb("var", [P, T]), sb("nt", [P, T])
        par = sb("par", [P, groups * P])
        ident, ones = sb("ident", [P, P]), sb("ones", [P, P])
        eps_c = sb("eps_c", [P, 1])
        dist = sb("dist", [P, TT, T])
        vbias, sinks = sb("vbias", [P, UC]), sb("sinks", [P, HEADS])
        pr = [sb(f"pr{i}", [P, TT, T]) for i in range(GROUP - 1)] + [ssum]
        prT = [cv, pad3[:, :, TAPS - 1:]]
        squares_of = pr[0:3] + [cv]
        rmax, nmax = sb("rmax", [P, GROUP, TT]), sb("nmax", [P, GROUP, TT])
        den, esink, rden = (sb(k, [P, GROUP, TT]) for k in ("den", "esink", "rden"))
        rstat = sb("rstat", [P, 6, TT])

        def flat(t):
            return t[:, :, :].rearrange("p a b -> p (a b)")
        x_rows = flat(memk[1]).rearrange("p (t d) -> p t d", t=TT)
        mem_rows = memv[1]
        par_rows = flat(memk[0])[:, 0:groups * P].rearrange("p (g c) -> p g c", c=P)
        out_rows = memv[0]
        wk, wks = memk[0][:, 0:2, :], memk[0][:, 2:4, :]
        wv = memk[0][:, 4:6, :]

        acc = [ps(f"acc{i}", [P, UB, T]) for i in range(SLOTS)]
        wide = [ps(f"wide{i}", [P, UB, T]) for i in range(NOUT)]
        stat = ps("stat", [P, UB, T])

        w_landed = [sem(f"w_landed{s}") for s in range(SLOTS)]
        hi_ready = sem("hi_ready")
        lo_ready = sem("lo_ready")
        unit_done = sem("unit_done")
        u_ready = sem("u_ready")
        glu_ready = sem("glu_ready")
        par_landed, x_landed, mem_landed = sem("par_landed"), sem("x_landed"), sem("mem_landed")
        bc_landed = sem("bc_landed")
        const_ready = sem("const_ready")
        rows_ready = sem("rows_ready")
        tr_done = sem("tr_done")
        tr_used = sem("tr_used")
        x_ready = sem("x_ready")
        sq_ready = sem("sq_ready")
        sum_ready = sem("sum_ready")
        stat_ready = sem("stat_ready")
        var_ready = sem("var_ready")
        r_ready = sem("r_ready")
        y_ready = sem("y_ready")
        yhi_ready = sem("yhi_ready")
        act_ready = sem("act_ready")
        gate_ready = sem("gate_ready")
        conv_ready = sem("conv_ready")
        silu_ready = sem("silu_ready")
        down_ready = sem("down_ready")
        qk_ready = sem("qk_ready")
        kv_ready = sem("kv_ready")
        score_done = sem("score_done")
        max_ready = sem("max_ready")
        exp_ready = sem("exp_ready")
        prob_ready = sem("prob_ready")
        pT_done = sem("pT_done")
        pT_ready = sem("pT_ready")
        pv_done = sem("pv_done")
        outT_ready = sem("outT_ready")
        stored = sem("stored")
        dve_chain, act_chain, pool_chain = sem("dve_chain"), sem("act_chain"), sem("pool_chain")

        def pc(key, r, parts=slice(None)):
            return par[parts, bass.ds(r + col[key], 1)]

        def pair(t, k):
            return t[:, 2 * k:2 * k + 2, :]

        block = ctx.enter_context(nc.Block())

        @block.sync
        def _(sp):
            def load(base, i, src):
                s = base % SLOTS
                if not isinstance(i, int) or base >= SLOTS:
                    sp.wait_ge(lo_ready, i * SLOTS + (base - SLOTS + 1))
                dst = raw[s][:, :, :] if src.shape[1] == KC else flat(raw[s]).rearrange("p (c n) -> p c n", n=D)
                sp.dma_start(dst, src).then_inc(w_landed[s], 16)

            def wcols(w, c0):
                return w[:, bass.ds(c0, UC)].rearrange("(c p) n -> p c n", p=P)

            def wrows(w, r0):
                return w[bass.ds(r0, UC), :].rearrange("(c p) n -> p c n", p=P)

            for st in stages:
                kind, n0 = st["kind"], st["n0"]
                if kind == "start":
                    for t in range(TT):
                        sp.dma_start(mem_rows[:, t, :], a["mem"][0, t * P:(t + 1) * P, :]).then_inc(mem_landed, 16)
                    for t in range(TT):
                        sp.dma_start(x_rows[:, t, :], a["x"][0, t * P:(t + 1) * P, :]).then_inc(x_landed, 16)
                elif kind == "memkv":
                    load(n0, 0, wcols(a["x_w_kv"][st["layer"]], st["k"] * UC))
                elif kind == "sconv":
                    w = a["a_w_in"][st["j"]]
                    with sp.Fori(1, NOUT + 1) as j1:
                        for u, part in enumerate((1, 2, 0)):
                            load(n0 + u - SLOTS, j1, wcols(w, j1 * UC + (part * D - UC)))
                elif kind in ("resid", "q"):
                    w = st["w"] if kind == "resid" else a["x_w_q"][st["layer"]]
                    for k in range(NOUT):
                        load(n0 + k, 0, wcols(w, k * UC))
                elif kind == "qkv":
                    for k in range(6):
                        load(n0 + k, 0, wcols(a["b_w_qkv"][0], k * UC))
                elif kind == "pw1":
                    for k in range(2 * NOUT):
                        load(n0 + k, 0, wcols(a["c_w_pw1"][0], (k % 2) * D + (k // 2) * UC))
                elif kind == "ffn":
                    w_up, w_down = a["f_w_up"][st["layer"]], a["f_w_down"][st["layer"]]
                    load(n0, 0, wcols(w_up, 0))
                    load(n0 + 1, 0, wcols(w_up, FF))
                    with sp.Fori(2, PAIRS + 1) as j1:
                        load(n0 - 1 - SLOTS, j1, wcols(w_up, j1 * UC + (-UC)))
                        load(n0 - SLOTS, j1, wrows(w_down, j1 * UC + (-2 * UC)))
                        load(n0 + 1 - SLOTS, j1, wcols(w_up, j1 * UC + (FF - UC)))
                elif kind == "down":
                    load(n0, 0, wrows(a["f_w_down"][st["layer"]], (PAIRS - 1) * UC))
            for g in range(2 * TT):
                t, half = divmod(g, 2)
                sp.wait_ge(outT_ready, g + 1)
                sp.dma_start(out[0, t * P:(t + 1) * P, half * 512:(half + 1) * 512],
                             out_rows[:, t, half * 512:(half + 1) * 512]).then_inc(stored, 16)
            sp.wait_ge(stored, 16 * 2 * TT)

        @block.gpsimd
        def _(pool):
            pool.dma_start(vbias[:, :], a["b_b_qkv"][0, (HEADS + KVH) * HD:].partition_broadcast(P)).then_inc(bc_landed, 16)
            pool.dma_start(sinks[:, :], a["b_sinks"][0].partition_broadcast(P)).then_inc(bc_landed, 16)
            chain = Chain(pool, pool_chain)
            pool.memset(ones[:, :], 1.0).then_inc(const_ready, 1)
            pool.memset(eps_c[:, :], EPS).then_inc(const_ready, 1)
            chain.link(pool.memset(ident[:, :], 0.0))
            pool.affine_select(out=ident[:, :], in_=ident[:, :], compare_op=ALU.not_equal, fill=1.0, base=0,
                               pattern=[[-1, P]], channel_multiplier=1).then_inc(const_ready, 1)
            chain.link(pool.iota(dist[:, :, :], [[P, TT], [-1, T]], base=0, channel_multiplier=1,
                                 allow_small_or_imprecise_dtypes=True))
            chain.link(pool.affine_select(out=dist[:, :, :], in_=dist[:, :, :], compare_op=ALU.is_ge, fill=FAR,
                                          base=0, pattern=[[P, TT], [-1, T]], channel_multiplier=1))
            pool.affine_select(out=dist[:, :, :], in_=dist[:, :, :], compare_op=ALU.is_ge, fill=FAR,
                               base=P - 1, pattern=[[-P, TT], [1, T]], channel_multiplier=-1).then_inc(const_ready, 1)

        CONSTS = 4

        @block.scalar
        def _(act):
            chain = Chain(act, act_chain)

            def split_hi(base, i):
                s = base % SLOTS
                act.wait_ge(w_landed[s], i * 16 + 16 * (base // SLOTS + 1))
                if base >= SLOTS:
                    act.wait_ge(unit_done, i * SLOTS + (base - SLOTS + 1))
                nc.scalar.activation(whi[s][:, :, :], raw[s][:, :, :], ACT.Copy).then_inc(hi_ready, 1)

            def ahead(base, i=0, last=False):
                if last is False or base + AHEAD + last * SLOTS < N:
                    split_hi(base + AHEAD, i)

            def y_hi(dst, slot, wait):
                act.wait_ge(y_ready, wait)
                nc.scalar.activation(dst, y[slot][:, :, :], ACT.Copy).then_inc(yhi_ready, 1)

            def square(k, wait):
                act.wait_ge(x_ready, wait)
                nc.scalar.activation(pair(inner, k), pair(x, k), ACT.Square).then_inc(sq_ready, 1)

            def rsqrt(wait):
                act.wait_ge(var_ready, wait)
                chain.link(nc.scalar.activation(nt[:, :], var[:, :], ACT.Ln))
                nc.scalar.activation(rs[:, :], nt[:, :], ACT.Exp, scale=-0.5).then_inc(r_ready, 1)

            for st in stages:
                kind, n0, c = st["kind"], st["n0"], st["c"]
                if kind == "start":
                    for g, p0, k, src in pieces:
                        act.dma_start(par_rows[p0:p0 + k, g, :], src).then_inc(par_landed, 16)
                    act.sem_inc(gate_ready, 1)
                    act.wait_ge(const_ready, CONSTS)
                    act.wait_ge(mem_landed, 16 * TT)
                    for t in range(TT):
                        e = nc.scalar.activation(memv[0][:, t, :], mem_rows[:, t, :], ACT.Square,
                                                 accum_out=rstat[:, 0, t:t + 1])
                    chain.link(e)
                    chain.link(nc.scalar.activation(rstat[:, 1, :], rstat[:, 0, :], ACT.Ln, bias=eps_c[:, 0:1],
                                                    scale=1.0 / D))
                    nc.scalar.activation(rstat[:, 2, :], rstat[:, 1, :], ACT.Exp, scale=-0.5).then_inc(r_ready, 1)
                    for k in range(NOUT):
                        square(k, k + 1)
                    for n in range(AHEAD):
                        split_hi(n, 0)
                elif kind == "mem_scale":
                    for k in range(NOUT):
                        y_hi(pair(g_hi, k), k % 2, c["y"] + k + 1)
                elif kind == "norm":
                    rsqrt(c["v"] + 1)
                    for k in range(NOUT):
                        y_hi(pair(h_hi, k), k % 2, c["y"] + k + 1)
                elif kind in ("memkv", "q", "qkv"):
                    for k in range(st["units"]):
                        ahead(n0 + k)
                elif kind == "sconv":
                    with act.Fori(0, NOUT) as j:
                        ahead(n0, j)
                        act.wait_ge(unit_done, j * 3 + (n0 + 1))
                        nc.scalar.activation(y[1][:, :, :], acc[n0 % SLOTS][:, :, :], ACT.Copy).then_inc(gate_ready, 1)
                        ahead(n0 + 1, j)
                        ahead(n0 + 2, j)
                        y_hi(m_hi[:, bass.ds(j * 2, 2), :], 0, j + (c["y"] + 1))
                elif kind == "resid":
                    for k in range(NOUT):
                        ahead(n0 + k)
                        square(k, c["x"] + k + 1)
                elif kind == "scores":
                    for h in range(GROUP):
                        act.wait_ge(max_ready, c["h"] + h + 1)
                        head = st["group"] * GROUP + h
                        src = wide[h] if st["layer"] is not None else pr[h]
                        if st["layer"] is None:
                            nc.scalar.activation(esink[:, h, :], nmax[:, h, :], ACT.Exp, bias=sinks[:, head:head + 1])
                        for q in range(TT):
                            e = nc.scalar.activation(pr[h][:, q, :], src[:, q, :], ACT.Exp, bias=nmax[:, h, q:q + 1],
                                                     accum_out=den[:, h, q:q + 1])
                        e.then_inc(exp_ready, 1)
                elif kind in ("attend", "swa_attend"):
                    for h in range(GROUP + 1):
                        if h < GROUP:
                            act.wait_ge(pT_done, c["hd"] + h + 1)
                            if c["hd"] + h >= 2:
                                act.wait_ge(pv_done, c["hd"] + h - 1)
                            nc.scalar.activation(prT[h % 2][:, :, :], wide[h][:, :, :], ACT.Copy).then_inc(pT_ready, 1)
                        if kind == "attend" and h >= 1:
                            y_hi(pair(m_hi, h - 1), (h - 1) % 2, c["y"] + h)
                    if kind == "swa_attend":
                        y_hi(pair(m_hi, st["group"]), 0, c["y"] + 1)
                elif kind == "pw1":
                    for k in range(2 * NOUT):
                        ahead(n0 + k)
                        if k % 2:
                            act.wait_ge(unit_done, n0 + k + 1)
                            if k > 1:
                                act.wait_ge(glu_ready, c["gl"] + k // 2)
                            for b in range(UB):
                                e = nc.scalar.activation(cv[:, b, :], acc[(n0 + k) % SLOTS][:, b, :], ACT.Sigmoid,
                                                         bias=pc("c_b_pw1", KC + k // 2 * UB + b))
                            e.then_inc(gate_ready, 1)
                elif kind == "lnorm":
                    for k in range(NOUT):
                        act.wait_ge(x_ready, c["x"] + k + 1)
                        nc.scalar.activation(squares_of[k][:, :, :], pair(inner, k), ACT.Square).then_inc(sq_ready, 1)
                    rsqrt(c["v"] + 1)
                    for k in range(NOUT):
                        act.wait_ge(conv_ready, c["c"] + k + 1)
                        if k >= 2:
                            act.wait_ge(act_ready, c["a"] + k - 1)
                        for b in range(UB):
                            e = nc.scalar.activation(y[k % 2][:, b, :], inner[:, 2 * k + b, :], ACT.Silu,
                                                     bias=pc("c_ln_b", 2 * k + b))
                        chain.link(e)
                        nc.scalar.activation(pair(m_hi, k), y[k % 2][:, :, :], ACT.Copy).then_inc(yhi_ready, 1)
                elif kind == "ffn":
                    def gate(bank, wait):
                        act.wait_ge(unit_done, wait)
                        nc.scalar.activation(pad3[:, :, TAPS - 1:], bank[:, :, :], ACT.Copy).then_inc(gate_ready, 1)

                    def silu(wait):
                        act.wait_ge(conv_ready, wait)
                        nc.scalar.activation(cv[:, :, :], cv[:, :, :], ACT.Silu).then_inc(silu_ready, 1)

                    def pair_of_units(j, last=False):
                        ahead(n0 - 1, j, last)
                        gate(acc[(n0 - 1) % SLOTS], j * 3 + n0)
                        ahead(n0, j, last)
                        silu(j + (c["c"] + 1))
                        ahead(n0 + 1, j, last)
                        y_hi(z_hi[:, :, :], 0, j + (c["y"] + 1))

                    ahead(n0)
                    gate(acc[n0 % SLOTS], n0 + 1)
                    ahead(n0 + 1)
                    silu(c["c"] + 1)
                    y_hi(z_hi[:, :, :], 0, c["y"] + 1)
                    with act.Fori(1, PAIRS - 1) as j:
                        pair_of_units(j)
                    pair_of_units(PAIRS - 1, PAIRS - 1)
                elif kind == "down":
                    ahead(n0, 0, 0)
                    for k in range(NOUT):
                        square(k, c["x"] + k + 1)
                elif kind == "final":
                    rsqrt(c["v"] + 1)

        @block.vector
        def _(dve):
            chain = Chain(dve, dve_chain)

            def split_lo(base, i):
                s = base % SLOTS
                dve.wait_ge(hi_ready, i * SLOTS + (base + 1))
                nc.vector.tensor_tensor(wlo[s][:, :, :], raw[s][:, :, :], whi[s][:, :, :].bitcast(F32),
                                        ALU.subtract).then_inc(lo_ready, 1)

            def ahead(base, i=0, last=False):
                if last is False or base + AHEAD + last * SLOTS < N:
                    split_lo(base + AHEAD, i)

            def y_lo(dst, hi, slot, wait):
                dve.wait_ge(yhi_ready, wait)
                nc.vector.tensor_tensor(dst, y[slot][:, :, :], hi.bitcast(F32), ALU.subtract).then_inc(act_ready, 1)

            def y_free(k, c):
                if c["a"] + max(k - 1, 0):
                    dve.wait_ge(act_ready, c["a"] + max(k - 1, 0))

            def sum_squares(k, src, wait):
                dve.wait_ge(sq_ready, wait)
                if k == 0:
                    return
                e = nc.vector.tensor_tensor(ssum[:, :, :], src(k), src(0) if k == 1 else ssum[:, :, :], ALU.add)
                if k == NOUT - 1:
                    e.then_inc(sum_ready, 1)
                else:
                    chain.link(e)

            def squares(k):
                return pair(inner, k)

            def refine(r, v, t, wait):
                dve.wait_ge(r_ready, wait)
                chain.link(nc.vector.tensor_tensor(t, r, r, ALU.mult))
                chain.link(nc.vector.tensor_tensor(t, t, v, ALU.mult))
                chain.link(nc.vector.tensor_scalar(t, t, -0.5, 1.5, ALU.mult, ALU.add))
                chain.link(nc.vector.tensor_tensor(r, r, t, ALU.mult))

            def inverse_rms(stat_wait, c):
                dve.wait_ge(stat_ready, stat_wait)
                nc.vector.tensor_scalar(var[:, :], stat[:, 0, :], 1.0 / D, EPS, ALU.mult, ALU.add).then_inc(var_ready, 1)
                dve.wait_ge(var_ready, c["v"] + 1)
                refine(rs[:, :], var[:, :], nt[:, :], c["r"] + 1)

            def scale_pair(dst, src, key, r0, k):
                for b in range(UB):
                    e = nc.vector.scalar_tensor_tensor(out=dst[:, b, :], in0=src[:, 2 * k + b, :],
                                                       scalar=pc(key, r0 + 2 * k + b), in1=rs[:, :],
                                                       op0=ALU.mult, op1=ALU.mult)
                return e

            def conv3(key, row):
                marks = [None] * UB
                for k in range(TAPS):
                    for b in range(UB):
                        src, w = pad3[:, b, k:k + T], pc(key, row(k, b))
                        if k == 0:
                            e = nc.vector.tensor_scalar(cv[:, b, :], src, w, None, ALU.mult)
                        else:
                            chain.wait(marks[b])
                            e = nc.vector.scalar_tensor_tensor(out=cv[:, b, :], in0=src, scalar=w, in1=cv[:, b, :],
                                                               op0=ALU.mult, op1=ALU.add)
                        if k < TAPS - 1:
                            marks[b] = chain.mark(e)
                return e

            CONV3 = UB * (TAPS - 1)

            def dwconv_part(part):
                j, q = divmod(part, CPARTS)
                marks = [chain.n] * UB
                for k in range(q * CSTEP, min(q * CSTEP + CSTEP, CTAPS)):
                    for b in range(UB):
                        ch = j * UB + b
                        src, w = mid[:, ch, k:k + T], pc("c_w_dw", k * KC + ch)
                        chain.wait(marks[b])
                        if k == 0:
                            e = nc.vector.tensor_scalar(pr[0][:, b, :], src, w, pc("c_b_dw", ch), ALU.mult, ALU.add)
                        else:
                            e = nc.vector.scalar_tensor_tensor(out=inner[:, ch, :] if k == CTAPS - 1 else pr[0][:, b, :],
                                                               in0=src, scalar=w, in1=pr[0][:, b, :],
                                                               op0=ALU.mult, op1=ALU.add)
                        marks[b] = chain.mark(e)

            def take_x(k, bank, bias):
                if bias is None:
                    e = nc.vector.tensor_tensor(pair(x, k), bank[:, :, :], pair(x, k), ALU.add)
                else:
                    for b in range(UB):
                        e = nc.vector.scalar_tensor_tensor(out=x[:, 2 * k + b, :], in0=bank[:, b, :],
                                                           scalar=pc(bias, 2 * k + b), in1=x[:, 2 * k + b, :],
                                                           op0=ALU.add, op1=ALU.add)
                e.then_inc(x_ready, 1)

            for st in stages:
                kind, n0, c = st["kind"], st["n0"], st["c"]
                if kind == "start":
                    nc.vector.memset(mid[:, :, 0:PAD], 0.0)
                    nc.vector.memset(pad3[:, :, 0:TAPS - 1], 0.0).then_inc(u_ready, 1)

                    def take(dst, src, g):
                        dve.wait_ge(tr_done, g + 1)
                        e = nc.vector.tensor_copy(dst, src)
                        e.then_inc(tr_used, 1)

                    take(par[:, 0:4 * P], flat(wide[0]), 0)
                    take(par[:, 4 * P:nrow], flat(wide[1])[:, 0:nrow - 4 * P], 1)
                    v, t = rstat[:, 3, :], rstat[:, 4, :]
                    dve.wait_ge(r_ready, 1)
                    chain.link(nc.vector.tensor_scalar(v, rstat[:, 0, :], 1.0 / D, EPS, ALU.mult, ALU.add))
                    refine(rstat[:, 2, :], v, t, 1)
                    for t in range(TT):
                        nc.vector.tensor_scalar(mem_rows[:, t, :], mem_rows[:, t, :], rstat[:, 2, t:t + 1], None,
                                                ALU.mult).then_inc(rows_ready, 1)
                    for k in range(NOUT):
                        dve.wait_ge(tr_done, 3 + k)
                        nc.vector.tensor_copy(pair(x, k), wide[(2 + k) % 4][:, :, :]).then_inc(x_ready, 1)
                    for n in range(AHEAD):
                        split_lo(n, 0)
                    for k in range(NOUT):
                        take(pair(memn, k), wide[(6 + k) % 4][:, :, :], 6 + k)
                    for k in range(NOUT):
                        sum_squares(k, squares, k + 1)
                elif kind == "mem_scale":
                    if st["layer"] == 0:
                        dve.wait_ge(tr_used, 6)
                    for k in range(NOUT):
                        y_free(k, c)
                        for b in range(UB):
                            e = nc.vector.tensor_scalar(y[k % 2][:, b, :], memn[:, 2 * k + b, :],
                                                        pc("norm_mem", st["layer"] * KC + 2 * k + b), None, ALU.mult)
                        e.then_inc(y_ready, 1)
                        if k:
                            y_lo(pair(g_lo, k - 1), pair(g_hi, k - 1), (k - 1) % 2, c["a"] + k)
                    y_lo(pair(g_lo, NOUT - 1), pair(g_hi, NOUT - 1), (NOUT - 1) % 2, c["a"] + NOUT)
                elif kind == "memkv":
                    ahead(n0)
                    dve.wait_ge(unit_done, n0 + 1)
                    k, i = st["k"], st["layer"] % 2
                    dst = pair(memk[i], k) if k < NOUT else memv[i][:, :, (k - NOUT) * UC:(k - NOUT + 1) * UC]
                    nc.vector.tensor_copy(dst, acc[n0 % SLOTS][:, :, :]).then_inc(kv_ready, 1)
                    if "part" in st:
                        dwconv_part(st["part"])
                elif kind == "norm":
                    inverse_rms(c["st"] + 1, c)
                    key, layer = st["g"]
                    for k in range(NOUT):
                        y_free(k, c)
                        scale_pair(y[k % 2], x, key, layer * KC, k).then_inc(y_ready, 1)
                        if k:
                            y_lo(pair(h_lo, k - 1), pair(h_hi, k - 1), (k - 1) % 2, c["a"] + k)
                    y_lo(pair(h_lo, NOUT - 1), pair(h_hi, NOUT - 1), (NOUT - 1) % 2, c["a"] + NOUT)
                elif kind == "sconv":
                    with dve.Fori(0, NOUT) as j:
                        chain.enter(j, CONV3 + 1)
                        ahead(n0, j)
                        ahead(n0 + 1, j)
                        dve.wait_ge(gate_ready, j + (c["g"] + 1))
                        dve.wait_ge(unit_done, j * 3 + (n0 + 2))
                        nc.vector.tensor_tensor(pad3[:, :, TAPS - 1:], acc[(n0 + 1) % SLOTS][:, :, :],
                                                y[1][:, :, :], ALU.mult).then_inc(u_ready, 1)
                        dve.wait_ge(u_ready, j + (c["u"] + 1))
                        conv = chain.mark(conv3("a_conv", lambda k, b: j * UB + (st["j"] * TAPS * KC + k * KC + b)))
                        ahead(n0 + 2, j)
                        dve.wait_ge(unit_done, j * 3 + (n0 + 3))
                        chain.wait(conv)
                        dve.wait_ge(act_ready, j + c["a"])
                        nc.vector.tensor_tensor(y[0][:, :, :], acc[(n0 + 2) % SLOTS][:, :, :], cv[:, :, :],
                                                ALU.mult).then_inc(y_ready, 1)
                        y_lo(m_lo[:, bass.ds(j * 2, 2), :], m_hi[:, bass.ds(j * 2, 2), :], 0, j + (c["a"] + 1))
                    chain.leave(NOUT)
                elif kind == "resid":
                    for k in range(NOUT):
                        ahead(n0 + k)
                        dve.wait_ge(unit_done, n0 + k + 1)
                        take_x(k, acc[(n0 + k) % SLOTS], st["bias"])
                        if k:
                            sum_squares(k - 1, squares, c["x"] + k)
                    sum_squares(NOUT - 1, squares, c["x"] + NOUT)
                elif kind == "down":
                    ahead(n0, 0, 0)
                    for k in range(NOUT):
                        if k < NOUT - 1:
                            dve.wait_ge(down_ready, c["d"] + k + 1)
                        else:
                            dve.wait_ge(unit_done, n0 + 1)
                        take_x(k, wide[k], None)
                        if k:
                            sum_squares(k - 1, squares, c["x"] + k)
                    sum_squares(NOUT - 1, squares, c["x"] + NOUT)
                elif kind == "q":
                    for k in range(NOUT):
                        ahead(n0 + k)
                        dve.wait_ge(unit_done, n0 + k + 1)
                        nc.vector.tensor_scalar(pair(inner, k), acc[(n0 + k) % SLOTS][:, :, :], XHD ** -0.5, None,
                                                ALU.mult).then_inc(qk_ready, 1)
                elif kind == "qkv":
                    for k in range(6):
                        ahead(n0 + k)
                        dve.wait_ge(unit_done, n0 + k + 1)
                        bank = acc[(n0 + k) % SLOTS]
                        if k < NOUT:
                            for b in range(UB):
                                e = nc.vector.tensor_scalar(inner[:, 2 * k + b, :], bank[:, b, :], pc("b_b_qkv", 2 * k + b),
                                                            HD ** -0.5, ALU.add, ALU.mult)
                        elif k == NOUT:
                            for b in range(UB):
                                e = nc.vector.tensor_scalar(wk[:, b, :], bank[:, b, :], pc("b_b_qkv", KC + b), None, ALU.add)
                            chain.link(e)
                            nc.vector.tensor_copy(wks[0:HD, :, :], wk[HD:P, :, :])
                            e = nc.vector.tensor_copy(wks[HD:P, :, :], wk[0:HD, :, :])
                        else:
                            dve.wait_ge(bc_landed, 32)
                            for b in range(TT):
                                e = nc.vector.tensor_tensor(wv[:, b, :], bank[:, b, :], vbias[:, :], ALU.add)
                        e.then_inc(qk_ready, 1)
                elif kind == "scores":
                    def normalise(h):
                        dve.wait_ge(exp_ready, c["h"] + h + 1)
                        if st["layer"] is None:
                            chain.link(nc.vector.tensor_tensor(den[:, h, :], den[:, h, :], esink[:, h, :], ALU.add))
                        chain.link(nc.vector.reciprocal(rden[:, h, :], den[:, h, :]))
                        for q in range(TT):
                            e = nc.vector.tensor_scalar(pr[h][:, q, :], pr[h][:, q, :], rden[:, h, q:q + 1], None, ALU.mult)
                        e.then_inc(prob_ready, 1)

                    for h in range(GROUP):
                        dve.wait_ge(score_done, c["h"] + h + 1)
                        if st["layer"] is None:
                            head = st["group"] * GROUP + h
                            slope = 2.0 ** (-8.0 * (head + 1) / HEADS)
                            chain.link(nc.vector.scalar_tensor_tensor(out=pr[h][:, :, :], in0=dist[:, :, :], scalar=-slope,
                                                                      in1=wide[h][:, :, :], op0=ALU.mult, op1=ALU.add))
                            chain.link(nc.vector.tensor_reduce(rmax[:, h, :], pr[h][:, :, :], AX_X, ALU.max))
                            nc.vector.tensor_scalar(nmax[:, h, :], rmax[:, h, :], sinks[:, head:head + 1], -1.0,
                                                    ALU.max, ALU.mult).then_inc(max_ready, 1)
                        else:
                            chain.link(nc.vector.tensor_reduce(rmax[:, h, :], wide[h][:, :, :], AX_X, ALU.max))
                            nc.vector.tensor_scalar(nmax[:, h, :], rmax[:, h, :], -1.0, None, ALU.mult).then_inc(max_ready, 1)
                        if h:
                            normalise(h - 1)
                    normalise(GROUP - 1)
                elif kind == "attend":
                    for h in range(XH):
                        dve.wait_ge(pv_done, c["hd"] + h + 1)
                        y_free(h, c)
                        nc.vector.tensor_copy(y[h % 2][:, :, :], wide[h][:, :, :]).then_inc(y_ready, 1)
                        if h:
                            y_lo(pair(m_lo, h - 1), pair(m_hi, h - 1), (h - 1) % 2, c["a"] + h)
                    y_lo(pair(m_lo, XH - 1), pair(m_hi, XH - 1), (XH - 1) % 2, c["a"] + XH)
                elif kind == "swa_attend":
                    g = st["group"]
                    dve.wait_ge(pv_done, c["hd"] + GROUP)
                    y_free(0, c)
                    nc.vector.tensor_copy(y[0][:, :, :], wide[0][:, :, :]).then_inc(y_ready, 1)
                    y_lo(pair(m_lo, g), pair(m_hi, g), 0, c["a"] + 1)
                elif kind == "pw1":
                    for k in range(2 * NOUT):
                        ahead(n0 + k)
                        if k % 2:
                            j = k // 2
                            dve.wait_ge(unit_done, n0 + k)
                            dve.wait_ge(gate_ready, c["g"] + j + 1)
                            for b in range(UB):
                                e = nc.vector.scalar_tensor_tensor(out=inner[:, 2 * j + b, :], in0=acc[(n0 + k - 1) % SLOTS][:, b, :],
                                                                   scalar=pc("c_b_pw1", 2 * j + b), in1=cv[:, b, :],
                                                                   op0=ALU.add, op1=ALU.mult)
                            e.then_inc(glu_ready, 1)
                            dve.wait_ge(glu_ready, c["gl"] + j + 1)
                        if k:
                            dwconv_part(k - 1)
                elif kind == "lnorm":
                    chain.wait(chain.n)
                    for k in range(1, NOUT):
                        e = nc.vector.tensor_tensor(ssum[:, :, :], pair(inner, k), pair(inner, 0) if k == 1 else ssum[:, :, :],
                                                    ALU.add)
                        if k < NOUT - 1:
                            chain.link(e)
                    e.then_inc(sum_ready, 1)
                    dve.wait_ge(stat_ready, c["st"] + 1)
                    chain.link(nc.vector.tensor_scalar(nt[:, :], stat[:, 0, :], 1.0 / D, None, ALU.mult))
                    for k in range(NOUT):
                        for b in range(UB):
                            e = nc.vector.tensor_tensor(inner[:, 2 * k + b, :], inner[:, 2 * k + b, :], nt[:, :], ALU.subtract)
                        e.then_inc(x_ready, 1)
                    for k in range(NOUT):
                        sum_squares(k, lambda k: squares_of[k][:, :, :], c["x"] + k + 1)
                    inverse_rms(c["st"] + 2, c)
                    for k in range(NOUT):
                        dve.wait_ge(x_ready, c["x"] + NOUT)
                        scale_pair(pair(inner, k), inner, "c_ln_g", 0, k).then_inc(conv_ready, 1)
                        if k:
                            y_lo(pair(m_lo, k - 1), pair(m_hi, k - 1), (k - 1) % 2, c["a"] + k)
                    y_lo(pair(m_lo, NOUT - 1), pair(m_hi, NOUT - 1), (NOUT - 1) % 2, c["a"] + NOUT)
                elif kind == "ffn":
                    def gate_conv(wait, j):
                        dve.wait_ge(gate_ready, wait)
                        conv3("f_conv", lambda k, b: j * UB + ((st["layer"] * TAPS + k) * FC + b)).then_inc(conv_ready, 1)

                    def up(wait, waits, waita):
                        dve.wait_ge(unit_done, wait)
                        dve.wait_ge(silu_ready, waits)
                        dve.wait_ge(act_ready, waita - 1)
                        nc.vector.tensor_tensor(y[0][:, :, :], acc[(n0 + 1) % SLOTS][:, :, :], cv[:, :, :],
                                                ALU.mult).then_inc(y_ready, 1)
                        y_lo(z_lo[:, :, :], z_hi[:, :, :], 0, waita)

                    def pair_of_units(j, last=False):
                        ahead(n0 - 1, j, last)
                        gate_conv(j + (c["g"] + 1), j)
                        ahead(n0, j, last)
                        ahead(n0 + 1, j, last)
                        up(j * 3 + (n0 + 2), j + (c["si"] + 1), j + (c["a"] + 1))

                    ahead(n0)
                    gate_conv(c["g"] + 1, 0)
                    ahead(n0 + 1)
                    up(n0 + 2, c["si"] + 1, c["a"] + 1)
                    with dve.Fori(1, PAIRS - 1) as j:
                        chain.enter(j - 1, CONV3)
                        pair_of_units(j)
                    chain.leave(PAIRS - 2)
                    pair_of_units(PAIRS - 1, PAIRS - 1)
                elif kind == "final":
                    inverse_rms(c["st"] + 1, c)
                    for k in range(NOUT):
                        scale_pair(pair(inner, k), x, "norm_final", 0, k).then_inc(conv_ready, 1)
                    for g in range(2 * TT):
                        t, half = divmod(g, 2)
                        dve.wait_ge(tr_done, c["tr"] + g + 1)
                        nc.vector.tensor_copy(out_rows[:, t, half * 512:(half + 1) * 512],
                                              flat(wide[g])).then_inc(outT_ready, 1)

        @block.tensor
        def _(pe):
            taken = [None] * SLOTS

            def bank_free(n, sem, value):
                if taken[n % SLOTS]:
                    pe.wait_ge(*taken[n % SLOTS])
                taken[n % SLOTS] = (sem, value)

            def products(out_, w, r, first, last):
                pe.matmul(out_, w[0], r[0], start=first, stop=False, skip_group_check=True)
                pe.matmul(out_, w[0], r[1], start=False, stop=False, skip_group_check=True)
                return pe.matmul(out_, w[1], r[0], start=False, stop=last, skip_group_check=True)

            def unit(base, i, operand, ready=None, tokens=False):
                s = base % SLOTS
                pe.wait_ge(lo_ready, i * SLOTS + (base + 1))
                for b in range(UB):
                    for kc in range(KC):
                        if ready is not None and b == 0 and kc % 2 == 0:
                            pe.wait_ge(act_ready, ready[kc // 2])
                        if tokens:
                            e = products(acc[s][:, b, :], [t[:, kc, b * P:(b + 1) * P] for t in operand],
                                         [whi[s][:, kc, :], wlo[s][:, kc, :]], kc == 0, kc == KC - 1)
                        else:
                            e = products(acc[s][:, b, :], [t[s][:, kc, b * P:(b + 1) * P] for t in (whi, wlo)],
                                         [t[:, kc, :] for t in operand], kc == 0, kc == KC - 1)
                e.then_inc(unit_done, 1)

            def down(base, i, ready, first, last):
                s = base % SLOTS
                pe.wait_ge(lo_ready, i * SLOTS + (base + 1))
                pe.wait_ge(act_ready, ready)
                w = [flat(t[s]).rearrange("p (c n) -> p c n", n=D) for t in (whi, wlo)]
                for nb in range(KC):
                    for kc in range(UB):
                        e = products(wide[nb // 2][:, nb % 2, :], [t[:, kc, nb * P:(nb + 1) * P] for t in w],
                                     [t[:, kc, :] for t in (z_hi, z_lo)], first and nb % 2 == 0 and kc == 0,
                                     last and kc == UB - 1)
                    if last and nb % 2 and nb < KC - 1:
                        e.then_inc(down_ready, 1)
                e.then_inc(unit_done, 1)

            def sum_features(wait):
                pe.wait_ge(sum_ready, wait)
                for b in range(UB):
                    e = pe.matmul(stat[:, 0, :], ones[:, :], ssum[:, b, :], start=(b == 0), stop=(b == UB - 1))
                e.then_inc(stat_ready, 1)

            H, M, G = (h_hi, h_lo), (m_hi, m_lo), (g_hi, g_lo)
            su = [0]
            made = {}
            for st in stages:
                kind, n0, c = st["kind"], st["n0"], st["c"]
                if kind == "start":
                    pe.wait_ge(const_ready, CONSTS)

                    def four(bank, srcs, g):
                        for q, src in enumerate(srcs):
                            e = pe.transpose(bank[:, q // 2, (q % 2) * P:(q % 2 + 1) * P], src, ident[0:src.shape[0], 0:src.shape[0]])
                        e.then_inc(tr_done, 1)
                    pe.wait_ge(par_landed, 16 * len(pieces))
                    rows = [min(P, nrow - g * P) for g in range(groups)]
                    for q in range(groups):
                        bank = wide[q // 4]
                        e = pe.transpose(bank[:, q % 4 // 2, (q % 2) * P:(q % 2) * P + rows[q]], par_rows[0:rows[q], q, :],
                                         ident[0:rows[q], 0:rows[q]])
                        if q in (3, groups - 1):
                            e.then_inc(tr_done, 1)
                    pe.wait_ge(x_landed, 16 * TT)
                    for k in range(NOUT):
                        if k >= 2:
                            pe.wait_ge(tr_used, k - 1)
                        four(wide[(2 + k) % 4], [x_rows[:, t, (2 * k + b) * P:(2 * k + b + 1) * P]
                                                 for b in range(UB) for t in range(TT)], 2 + k)
                    pe.wait_ge(rows_ready, TT)
                    for k in range(NOUT):
                        pe.wait_ge(x_ready, k + 1)
                        four(wide[(6 + k) % 4], [mem_rows[:, t, (2 * k + b) * P:(2 * k + b + 1) * P]
                                                 for b in range(UB) for t in range(TT)], 6 + k)
                elif kind == "memkv":
                    k = st["k"]
                    bank_free(n0, kv_ready, c["kv"] + 1)
                    unit(n0, 0, G, ready=made["g"] if k == 0 else None, tokens=k >= NOUT)
                elif kind == "norm":
                    su[0] += 1
                    sum_features(su[0])
                    made["h"] = [c["a"] + k + 1 for k in range(NOUT)]
                elif kind == "sconv":
                    by = ((gate_ready, c["g"]), (u_ready, c["u"]), (y_ready, c["y"]))
                    for u in range(3):
                        bank_free(n0 + u, by[u][0], by[u][1] + NOUT)
                    pe.wait_ge(act_ready, made["h"][-1])
                    with pe.Fori(0, NOUT) as j:
                        for u in range(3):
                            pe.wait_ge(by[u][0], j + by[u][1])
                            unit(n0 + u, j, H)
                    made["m"] = [c["a"] + k + 1 for k in range(NOUT)]
                elif kind in ("resid", "q", "qkv", "pw1"):
                    for k in range(st["units"]):
                        if kind == "resid":
                            bank_free(n0 + k, x_ready, c["x"] + k + 1)
                        elif kind == "pw1":
                            bank_free(n0 + k, *((gate_ready, c["g"] + k // 2 + 1) if k % 2
                                                else (glu_ready, c["gl"] + k // 2 + 1)))
                        else:
                            bank_free(n0 + k, qk_ready, c["q"] + k + 1)
                        if kind == "resid":
                            unit(n0 + k, 0, M, ready=made["m"] if k == 0 else None)
                        else:
                            unit(n0 + k, 0, H, ready=made["h"] if k == 0 else None, tokens=(kind == "qkv" and k == 5))
                elif kind == "scores":
                    pe.wait_ge(qk_ready, c["q"])
                    if st["layer"] is not None:
                        i = st["layer"] % 2
                        pe.wait_ge(kv_ready, 2 * NOUT * st["layer"] + NOUT)
                    elif st["group"]:
                        pe.wait_ge(y_ready, c["y"])
                    for h in range(GROUP):
                        for q in range(TT):
                            if st["layer"] is not None:
                                for kc in range(UB):
                                    e = pe.matmul(wide[h][:, q, :], inner[:, UB * h + kc, q * P:(q + 1) * P],
                                                  memk[i][:, UB * h + kc, :], start=(kc == 0), stop=(kc == UB - 1))
                            else:
                                head = st["group"] * GROUP + h
                                kv = head // (HEADS // KVH)
                                half = slice(head % 2 * HD, head % 2 * HD + HD)
                                keys = wk if kv % 2 == head % 2 else wks
                                e = pe.matmul(wide[h][:, q, :], inner[half, head // 2, q * P:(q + 1) * P],
                                              keys[half, kv // 2, :], start=True, stop=True)
                        e.then_inc(score_done, 1)
                elif kind in ("attend", "swa_attend"):
                    def transpose_head(h):
                        pe.wait_ge(prob_ready, c["hd"] + h + 1)
                        for kk in range(TT):
                            for q in range(TT):
                                e = pe.transpose(wide[h][:, kk, q * P:(q + 1) * P], pr[h][:, q, kk * P:(kk + 1) * P], ident[:, :])
                        e.then_inc(pT_done, 1)

                    def values(h):
                        pe.wait_ge(pT_ready, c["hd"] + h + 1)
                        if kind == "attend":
                            i = st["layer"] % 2
                            for b in range(UB):
                                for kk in range(TT):
                                    e = pe.matmul(wide[h][:, b, :], memv[i][:, kk, h * XHD + b * P:h * XHD + (b + 1) * P],
                                                  prT[h % 2][:, kk, :], start=(kk == 0), stop=(kk == TT - 1))
                        else:
                            kv = st["group"] * GROUP // (HEADS // KVH)
                            half = slice(h % 2 * HD, h % 2 * HD + HD)
                            for kk in range(TT):
                                e = pe.matmul(wide[0][half, h // 2, :], wv[:, kk, kv * HD:(kv + 1) * HD],
                                              prT[h % 2][:, kk, :], start=(kk == 0), stop=(kk == TT - 1), skip_group_check=True)
                        e.then_inc(pv_done, 1)

                    if kind == "attend":
                        pe.wait_ge(kv_ready, 2 * NOUT * (st["layer"] + 1))
                        made["m"] = [c["a"] + k + 1 for k in range(NOUT)]
                    else:
                        made["m"] = made["m"][:st["group"]] + [c["a"] + 1] if st["group"] else [c["a"] + 1]
                    transpose_head(0)
                    for h in range(1, GROUP):
                        transpose_head(h)
                        values(h - 1)
                    values(GROUP - 1)
                elif kind == "mem_scale":
                    made["g"] = [c["a"] + k + 1 for k in range(NOUT)]
                elif kind == "lnorm":
                    made["m"] = [c["a"] + k + 1 for k in range(NOUT)]
                    for _ in range(2):
                        su[0] += 1
                        sum_features(su[0])
                elif kind == "ffn":
                    g0, y0, a0 = c["g"], c["y"], c["a"]
                    bank_free(n0, gate_ready, g0 + 1)
                    unit(n0, 0, H, ready=made["h"])
                    bank_free(n0 + 1, y_ready, y0 + PAIRS)
                    unit(n0 + 1, 0, H)

                    def pair_of_units(j, first=False):
                        pe.wait_ge(gate_ready, j + g0)
                        unit(n0 - 1, j, H)
                        down(n0, j, j + a0, first, False)
                        pe.wait_ge(y_ready, j + y0)
                        unit(n0 + 1, j, H)

                    bank_free(n0 + 2, gate_ready, g0 + PAIRS)
                    pair_of_units(1, True)
                    with pe.Fori(2, PAIRS) as j:
                        pair_of_units(j)
                    z_ready = a0 + PAIRS
                elif kind == "down":
                    down(n0, 0, z_ready, False, True)
                elif kind == "final":
                    su[0] += 1
                    sum_features(su[0])
                    for g in range(2 * TT):
                        t, half = divmod(g, 2)
                        pe.wait_ge(conv_ready, c["c"] + 2 * half + 2)
                        for q in range(4):
                            e = pe.transpose(wide[g][:, q // 2, (q % 2) * P:(q % 2 + 1) * P],
                                             inner[:, half * 4 + q, t * P:(t + 1) * P], ident[:, :])
                        e.then_inc(tr_done, 1)


_INS = ["x", "mem", "norm_mix", "norm_xattn", "norm_mem", "norm_ffn", "norm_final",
        "a_w_in", "a_conv", "a_w_out",
        "b_w_qkv", "b_b_qkv", "b_sinks", "b_w_o", "b_b_o",
        "c_w_pw1", "c_b_pw1", "c_w_dw", "c_b_dw", "c_ln_g", "c_ln_b", "c_w_pw2", "c_b_pw2",
        "x_w_q", "x_w_kv", "x_w_o", "f_w_up", "f_conv", "f_w_down"]


def kernel(**inputs):
    import numpy as _np
    import concourse.bacc as _bacc
    from concourse import mybir as _mybir
    from concourse.bass_utils import run_bass_kernel_spmd as _run

    nc = _bacc.Bacc("TRN2", target_bir_lowering=False, num_devices=1)
    arrays, aps = {}, {}
    for name in _INS:
        v = _np.ascontiguousarray(inputs[name])
        arrays[f"in_{name}"] = v
        aps[name] = nc.dram_tensor(f"in_{name}", v.shape, _mybir.dt.from_np(v.dtype), kind="ExternalInput").ap()
    out = nc.dram_tensor("out", (1, T, D), F32, kind="ExternalOutput").ap()
    build(nc, aps, out)
    r = _run(nc, [arrays], core_ids=[0])
    return r.results[0]["out"]
```

```python
from contextlib import ExitStack

import concourse.bass as bass
from concourse import mybir

ALU = mybir.AluOpType
ACT = mybir.ActivationFunctionType
AX_X = mybir.AxisListType.X
F32 = mybir.dt.float32
F32R = mybir.dt.float32r

P = 128
D = 1024
T = 256
DEPTH = 4
KC = D // P
TT = T // P
FF = 2816
FC = FF // P
UC = 256
UB = UC // P
PAIRS = FF // UC
NOUT = D // UC
SLOTS = 3
TAPS = 3
CTAPS = 31
HEADS = 16
KVH = 4
HD = 64
XH = 4
XHD = D // XH
PAD = CTAPS - 1
CPARTS = 4
CSTEP = -(-CTAPS // CPARTS)
GROUP = 4
EPS = 1e-6
FAR = 1e30




ADDS = {
    "start": dict(x=4, su=1, r=1, tr=11, g=1, u=1, a=4, y=4),
    "mem_scale": dict(a=4, y=4),
    "memkv": dict(kv=1),
    "norm": dict(a=4, y=4, st=1, v=1, r=1),
    "sconv": dict(a=4, y=4, g=4, u=4, st=1, v=1, r=1),
    "resid": dict(x=4, su=1),
    "q": dict(q=4, st=1, v=1, r=1),
    "qkv": dict(q=6),
    "scores": dict(h=GROUP),
    "attend": dict(a=XH, y=XH, hd=GROUP),
    "swa_attend": dict(a=1, y=1, hd=GROUP),
    "pw1": dict(sg=4, gl=4),
    "lnorm": dict(a=4, x=4, su=2, st=2, v=1, r=1, c=4),
    "ffn": dict(st=1, v=1, r=1, a=PAIRS, y=PAIRS, g=PAIRS, c=PAIRS, si=PAIRS),
    "down": dict(x=4, su=1, d=3),
    "final": dict(st=1, v=1, r=1, c=4, tr=4),
}


class Chain:

    def __init__(self, eng, sem):
        self.eng, self.sem, self.n, self.i, self.per = eng, sem, 0, 0, 0

    def mark(self, ins):
        self.n += 1
        ins.then_inc(self.sem, 1)
        return self.n

    def wait(self, mark):
        self.eng.wait_ge(self.sem, mark if self.per == 0 else self.i * self.per + mark)

    def link(self, ins):
        self.wait(self.mark(ins))

    def enter(self, i, per):
        self.i, self.per, self.start = i, per, self.n

    def leave(self, trips):
        assert self.n - self.start == self.per, (self.n - self.start, self.per)
        self.n = self.start + trips * self.per
        self.i = self.per = 0



STAGES = []


def matmuls(st):
    kv = st["kind"]
    return {"memkv": 50 if st["n0"]==0 else 48, "sconv": 576+4, "resid": 192, "q": 192+4, "qkv": 288, "scores": 32 if st.get("layer") is not None else 16,
            "attend": 48, "swa_attend": 28, "pw1": 384, "lnorm": 8, "norm": 4, "ffn": 32 * 48+4, "down": 48, "start": 38,
            "final": 20, "mem_scale": 0}[kv]


def build(nc, a, out):
    params = [
        ("norm_mem", a["norm_mem"].rearrange("i (c p) -> (i c) p", p=P)),
        ("norm_mix", a["norm_mix"].rearrange("i (c p) -> (i c) p", p=P)),
        ("norm_xattn", a["norm_xattn"].rearrange("i (c p) -> (i c) p", p=P)),
        ("norm_ffn", a["norm_ffn"].rearrange("i (c p) -> (i c) p", p=P)),
        ("a_conv", a["a_conv"].rearrange("j k (c p) -> (j k c) p", p=P)),
        ("norm_final", a["norm_final"].rearrange("(c p) -> c p", p=P)),
        ("b_b_qkv", a["b_b_qkv"].rearrange("j (c p) -> (j c) p", p=P)),
        ("b_b_o", a["b_b_o"].rearrange("j (c p) -> (j c) p", p=P)),
        ("c_b_pw1", a["c_b_pw1"].rearrange("j (c p) -> (j c) p", p=P)),
        ("c_b_dw", a["c_b_dw"].rearrange("j (c p) -> (j c) p", p=P)),
        ("c_ln_g", a["c_ln_g"].rearrange("j (c p) -> (j c) p", p=P)),
        ("c_ln_b", a["c_ln_b"].rearrange("j (c p) -> (j c) p", p=P)),
        ("c_b_pw2", a["c_b_pw2"].rearrange("j (c p) -> (j c) p", p=P)),
        ("f_conv", a["f_conv"].rearrange("i k (c p) -> (i k c) p", p=P)),
        ("c_w_dw", a["c_w_dw"].rearrange("j k (c p) -> (j k c) p", p=P)),
    ]
    col, nrow = {}, 0
    for key, ap in params:
        col[key] = nrow
        nrow += ap.shape[0]
    groups = -(-nrow // P)
    pieces = []
    for key, ap in params:
        r = 0
        while r < ap.shape[0]:
            g, p0 = divmod(col[key] + r, P)
            k = min(ap.shape[0] - r, P - p0)
            pieces.append((g, p0, k, ap[r:r + k, :]))
            r += k

    stages = []
    counts = dict(n=0)

    def stage(kind, units=0, **kw):
        stages.append(dict(kind=kind, n0=counts["n"], units=units, c=dict(counts), **kw))
        counts["n"] += units
        for key, v in ADDS[kind].items():
            counts[key] = counts.get(key, 0) + v
        if kw.get("next_g"):
            counts["a"] += NOUT
            counts["y"] += NOUT

    for adds in ADDS.values():
        for key in adds:
            counts.setdefault(key, 0)
    filled = [0]

    def fill(count):
        for _ in range(count):
            layer, k = divmod(filled[0], 2 * NOUT)
            stage("memkv", 1, layer=layer, k=k)
            filled[0] += 1

    def mem_scale(layer):
        assert filled[0] == 2 * NOUT * layer
        stage("mem_scale", layer=layer)

    def shortconv(layer, j):
        stage("sconv", 3 * NOUT, j=j)
        stage("resid", NOUT, w=a["a_w_out"][j], bias=None, next_g=("norm_xattn", layer))

    def xattn(layer, f_softmax, scale_for=None):
        stage("q", NOUT, layer=layer)
        stage("scores", layer=layer, group=0)
        fill(f_softmax)
        stage("attend", layer=layer, group=0)
        if scale_for:
            mem_scale(scale_for)
        stage("resid", NOUT, w=a["x_w_o"][layer], bias=None, next_g=("norm_ffn", layer))

    def ffn(layer, f_down, f_norm, next_g=None):
        stage("ffn", 3 * PAIRS - 1, layer=layer)
        fill(f_down)
        stage("down", 1, layer=layer, next_g=next_g)
        fill(f_norm)

    stage("start", next_g=("norm_mix", 0))
    fill(6)
    shortconv(0, 0)
    xattn(0, 2, scale_for=1)
    ffn(0, 0, 1)
    stage("norm", g=("norm_mix", 1))
    fill(1)
    stage("qkv", 6)
    for group in range(HEADS // GROUP):
        stage("scores", layer=None, group=group)
        fill(1)
        stage("swa_attend", layer=None, group=group)
    stage("resid", NOUT, w=a["b_w_o"][0], bias="b_b_o", next_g=("norm_xattn", 1))
    xattn(1, 2, scale_for=2)
    ffn(1, 1, 1)
    stage("norm", g=("norm_mix", 2))
    fill(1)
    stage("pw1", 2 * NOUT)
    part = 2 * NOUT - 1
    for k in range(8):
        if filled[0] == 2 * NOUT * 3:
            mem_scale(3)
        fill(1)
        stages[-1]["part"] = part
        part += 1
    stage("lnorm", part=part)
    assert part == CPARTS * NOUT - 1
    stage("resid", NOUT, w=a["c_w_pw2"][0], bias="c_b_pw2", next_g=("norm_xattn", 2))
    xattn(2, 2)
    ffn(2, 0, 1, next_g=("norm_mix", 3))
    shortconv(3, 1)
    xattn(3, 2)
    ffn(3, 0, 0)
    stage("final")
    assert filled[0] == 2 * NOUT * DEPTH
    N = counts["n"]
    STAGES[:] = stages

    with ExitStack() as ctx:
        def sb(name, shape, dt=F32):
            return ctx.enter_context(nc.sbuf_tensor(name, shape, dt))

        def ps(name, shape):
            return ctx.enter_context(nc.psum_tensor(name, shape, F32))

        def sem(name):
            return ctx.enter_context(nc.semaphore(name))

        raw = [sb(f"raw{s}", [P, KC, UC]) for s in range(SLOTS)]
        whi = [sb(f"whi{s}", [P, KC, UC], F32R) for s in range(SLOTS)]
        wlo = [sb(f"wlo{s}", [P, KC, UC], F32R) for s in range(SLOTS)]
        x = sb("x", [P, KC, T])
        h_hi, h_lo = sb("h_hi", [P, KC, T], F32R), sb("h_lo", [P, KC, T], F32R)
        m_hi, m_lo = sb("m_hi", [P, KC, T], F32R), sb("m_lo", [P, KC, T], F32R)
        z_hi, z_lo = sb("z_hi", [P, UB, T], F32R), sb("z_lo", [P, UB, T], F32R)
        memt = sb("memt", [P, KC, T])
        g_hi, g_lo = sb("g_hi", [P, KC, T], F32R), sb("g_lo", [P, KC, T], F32R)
        memk = [sb(f"memk{i}", [P, KC, T]) for i in range(2)]
        memv = [sb(f"memv{i}", [P, TT, D]) for i in range(2)]
        mid = sb("mid", [P, KC, PAD + T])
        inner = mid[:, :, PAD:PAD + T]
        pad3 = sb("pad3", [P, UB, TAPS - 1 + T])
        cv = sb("cv", [P, UB, T])
        y = [sb(f"y{i}", [P, UB, T]) for i in range(2)]
        ssum = sb("ssum", [P, UB, T])
        rs, var, nt = sb("rs", [P, T]), sb("var", [P, T]), sb("nt", [P, T])
        rs_mem = sb("rs_mem", [P, T])
        par = sb("par", [P, groups * P])
        ident, ones = sb("ident", [P, P]), sb("ones", [P, P])
        eps_c = sb("eps_c", [P, 1])
        dist = sb("dist", [P, TT, T])
        sinks = sb("sinks", [P, HEADS])
        pr = [sb(f"pr{i}", [P, TT, T]) for i in range(GROUP - 1)] + [ssum]
        prT = [cv, pad3[:, :, TAPS - 1:]]
        squares_of = pr[0:3] + [cv]
        rmax, nmax = sb("rmax", [P, GROUP, TT]), sb("nmax", [P, GROUP, TT])
        den, esink, rden = (sb(k, [P, GROUP, TT]) for k in ("den", "esink", "rden"))
        rstat = sb("rstat", [P, 6, TT])

        def both(t):
            return t[:, :].unsqueeze(1).broadcast_to([P, UB, T])

        def flat(t):
            return t[:, :, :].rearrange("p a b -> p (a b)")
        x_rows = flat(memk[1]).rearrange("p (t d) -> p t d", t=TT)
        mem_rows = memv[1]
        par_rows = flat(memk[0])[:, 0:groups * P].rearrange("p (g c) -> p g c", c=P)
        out_rows = memv[0]
        wk, wks = memk[0][:, 0:2, :], memk[0][:, 2:4, :]
        wv, vbias = memk[0][:, 4:6, :], memk[0][:, 6, :]

        acc = [ps(f"acc{i}", [P, UB, T]) for i in range(SLOTS)]
        wide = [ps(f"wide{i}", [P, UB, T]) for i in range(NOUT)]
        stat = ps("stat", [P, UB, T])

        w_landed = [sem(f"w_landed{s}") for s in range(SLOTS)]
        hi_ready = sem("hi_ready")
        lo_ready = sem("lo_ready")
        unit_done = sem("unit_done")
        u_ready = sem("u_ready")
        glu_ready = sem("glu_ready")
        par_landed, x_landed, mem_landed = sem("par_landed"), sem("x_landed"), sem("mem_landed")
        bc_landed = sem("bc_landed")
        const_ready = sem("const_ready")
        rows_ready = sem("rows_ready")
        rsm_ready = sem("rsm_ready")
        tr_done = sem("tr_done")
        tr_used = sem("tr_used")
        x_ready = sem("x_ready")
        sq_ready = sem("sq_ready")
        sum_ready = sem("sum_ready")
        stat_ready = sem("stat_ready")
        var_ready = sem("var_ready")
        r_ready = sem("r_ready")
        y_ready = sem("y_ready")
        yhi_ready = sem("yhi_ready")
        act_ready = sem("act_ready")
        gate_ready = sem("gate_ready")
        sig_ready = sem("sig_ready")
        conv_ready = sem("conv_ready")
        silu_ready = sem("silu_ready")
        down_ready = sem("down_ready")
        qk_ready = sem("qk_ready")
        kv_ready = sem("kv_ready")
        score_done = sem("score_done")
        max_ready = sem("max_ready")
        exp_ready = sem("exp_ready")
        prob_ready = sem("prob_ready")
        pT_done = sem("pT_done")
        pT_ready = sem("pT_ready")
        pv_done = sem("pv_done")
        outT_ready = sem("outT_ready")
        stored = sem("stored")
        dve_chain, act_chain, pool_chain = sem("dve_chain"), sem("act_chain"), sem("pool_chain")

        def pc(key, r, parts=slice(None)):
            return par[parts, bass.ds(r + col[key], 1)]

        def pair(t, k):
            return t[:, 2 * k:2 * k + 2, :]

        block = ctx.enter_context(nc.Block())

        @block.sync
        def _(sp):
            def load(base, i, src):
                s = base % SLOTS
                if not isinstance(i, int) or base >= SLOTS:
                    sp.wait_ge(lo_ready, i * SLOTS + (base - SLOTS + 1))
                dst = raw[s][:, :, :] if src.shape[1] == KC else flat(raw[s]).rearrange("p (c n) -> p c n", n=D)
                sp.dma_start(dst, src).then_inc(w_landed[s], 16)

            def wcols(w, c0):
                return w[:, bass.ds(c0, UC)].rearrange("(c p) n -> p c n", p=P)

            def wrows(w, r0):
                return w[bass.ds(r0, UC), :].rearrange("(c p) n -> p c n", p=P)

            for st in stages:
                kind, n0 = st["kind"], st["n0"]
                if kind == "start":
                    for t in range(TT):
                        sp.dma_start(mem_rows[:, t, :], a["mem"][0, t * P:(t + 1) * P, :]).then_inc(mem_landed, 16)
                    for t in range(TT):
                        sp.dma_start(x_rows[:, t, :], a["x"][0, t * P:(t + 1) * P, :]).then_inc(x_landed, 16)
                    sp.wait_ge(par_landed, 16 * len(pieces))
                elif kind == "memkv":
                    load(n0, 0, wcols(a["x_w_kv"][st["layer"]], st["k"] * UC))
                elif kind == "sconv":
                    w = a["a_w_in"][st["j"]]
                    with sp.Fori(1, NOUT + 1) as j1:
                        for u, part in enumerate((1, 2, 0)):
                            load(n0 + u - SLOTS, j1, wcols(w, j1 * UC + (part * D - UC)))
                elif kind in ("resid", "q"):
                    w = st["w"] if kind == "resid" else a["x_w_q"][st["layer"]]
                    for k in range(NOUT):
                        load(n0 + k, 0, wcols(w, k * UC))
                elif kind == "qkv":
                    for k in range(6):
                        load(n0 + k, 0, wcols(a["b_w_qkv"][0], k * UC))
                elif kind == "pw1":
                    for k in range(2 * NOUT):
                        load(n0 + k, 0, wcols(a["c_w_pw1"][0], (k % 2) * D + (k // 2) * UC))
                elif kind == "ffn":
                    w_up, w_down = a["f_w_up"][st["layer"]], a["f_w_down"][st["layer"]]
                    load(n0, 0, wcols(w_up, 0))
                    load(n0 + 1, 0, wcols(w_up, FF))
                    with sp.Fori(2, PAIRS + 1) as j1:
                        load(n0 - 1 - SLOTS, j1, wcols(w_up, j1 * UC + (-UC)))
                        load(n0 - SLOTS, j1, wrows(w_down, j1 * UC + (-2 * UC)))
                        load(n0 + 1 - SLOTS, j1, wcols(w_up, j1 * UC + (FF - UC)))
                elif kind == "down":
                    load(n0, 0, wrows(a["f_w_down"][st["layer"]], (PAIRS - 1) * UC))
            for g in range(2 * TT):
                t, half = divmod(g, 2)
                sp.wait_ge(outT_ready, g + 1)
                sp.dma_start(out[0, t * P:(t + 1) * P, half * 512:(half + 1) * 512],
                             out_rows[:, t, half * 512:(half + 1) * 512]).then_inc(stored, 16)
            sp.wait_ge(stored, 16 * 2 * TT)

        @block.gpsimd
        def _(pool):
            pool.dma_start(sinks[:, :], a["b_sinks"][0].partition_broadcast(P)).then_inc(bc_landed, 16)
            chain = Chain(pool, pool_chain)
            pool.memset(ones[:, :], 1.0).then_inc(const_ready, 1)
            pool.memset(eps_c[:, :], EPS).then_inc(const_ready, 1)
            chain.link(pool.memset(ident[:, :], 0.0))
            pool.affine_select(out=ident[:, :], in_=ident[:, :], compare_op=ALU.not_equal, fill=1.0, base=0,
                               pattern=[[-1, P]], channel_multiplier=1).then_inc(const_ready, 1)
            chain.link(pool.iota(dist[:, :, :], [[P, TT], [-1, T]], base=0, channel_multiplier=1,
                                 allow_small_or_imprecise_dtypes=True))
            chain.link(pool.affine_select(out=dist[:, :, :], in_=dist[:, :, :], compare_op=ALU.is_ge, fill=FAR,
                                          base=0, pattern=[[P, TT], [-1, T]], channel_multiplier=1))
            pool.affine_select(out=dist[:, :, :], in_=dist[:, :, :], compare_op=ALU.is_ge, fill=FAR,
                               base=P - 1, pattern=[[-P, TT], [1, T]], channel_multiplier=-1).then_inc(const_ready, 1)
            pool.wait_ge(pv_done, XH)
            pool.dma_start(vbias, a["b_b_qkv"][0, (HEADS + KVH) * HD:].partition_broadcast(P)).then_inc(bc_landed, 16)

        CONSTS = 4

        @block.scalar
        def _(act):
            chain = Chain(act, act_chain)

            def split_hi(base, i):
                s = base % SLOTS
                act.wait_ge(w_landed[s], i * 16 + 16 * (base // SLOTS + 1))
                if base >= SLOTS:
                    act.wait_ge(unit_done, i * SLOTS + (base - SLOTS + 1))
                nc.scalar.activation(whi[s][:, :, :], raw[s][:, :, :], ACT.Copy).then_inc(hi_ready, 1)

            def after(base, i=0):
                if not isinstance(i, int) or base + (i + 1) * SLOTS < N:
                    split_hi(base + SLOTS, i)

            def y_hi(dst, slot, wait):
                act.wait_ge(y_ready, wait)
                nc.scalar.activation(dst, y[slot][:, :, :], ACT.Copy).then_inc(yhi_ready, 1)

            def square(k, wait):
                act.wait_ge(x_ready, wait)
                nc.scalar.activation(pair(inner, k), pair(x, k), ACT.Square).then_inc(sq_ready, 1)

            def rsqrt(wait):
                act.wait_ge(var_ready, wait)
                chain.link(nc.scalar.activation(nt[:, :], var[:, :], ACT.Ln))
                nc.scalar.activation(rs[:, :], nt[:, :], ACT.Exp, scale=-0.5).then_inc(r_ready, 1)

            for st in stages:
                kind, n0, c = st["kind"], st["n0"], st["c"]
                if kind == "start":
                    for g, p0, k, src in pieces:
                        act.dma_start(par_rows[p0:p0 + k, g, :], src).then_inc(par_landed, 16)
                    act.wait_ge(const_ready, CONSTS)
                    act.wait_ge(mem_landed, 16 * TT)
                    for t in range(TT):
                        e = nc.scalar.activation(memv[0][:, t, :], mem_rows[:, t, :], ACT.Square,
                                                 accum_out=rstat[:, 0, t:t + 1])
                    chain.link(e)
                    chain.link(nc.scalar.activation(rstat[:, 1, :], rstat[:, 0, :], ACT.Ln, bias=eps_c[:, 0:1],
                                                    scale=1.0 / D))
                    nc.scalar.activation(rstat[:, 2, :], rstat[:, 1, :], ACT.Exp, scale=-0.5).then_inc(r_ready, 1)
                    for k in range(NOUT):
                        y_hi(pair(g_hi, k), k % 2, k + 1)
                    for n in range(SLOTS):
                        split_hi(n, 0)
                    for k in range(NOUT):
                        square(k, k + 1)
                        y_hi(pair(h_hi, k), k % 2, NOUT + k + 1)
                elif kind == "mem_scale":
                    for k in range(NOUT):
                        y_hi(pair(g_hi, k), k % 2, c["y"] + k + 1)
                elif kind == "norm":
                    rsqrt(c["v"] + 1)
                    for k in range(NOUT):
                        y_hi(pair(h_hi, k), k % 2, c["y"] + k + 1)
                elif kind in ("memkv", "q", "qkv"):
                    for k in range(st["units"]):
                        if kind == "q" and k == 0:
                            rsqrt(c["v"] + 1)
                        after(n0 + k)
                elif kind == "sconv":
                    rsqrt(c["v"] + 1)
                    with act.Fori(0, NOUT) as j:
                        after(n0, j)
                        after(n0 + 1, j)
                        y_hi(m_hi[:, bass.ds(j * 2, 2), :], 0, j + (c["y"] + 1))
                        after(n0 + 2, j)
                elif kind == "resid":
                    for k in range(NOUT):
                        if k < NOUT - 1:
                            after(n0 + k)
                        y_hi(pair(h_hi, k), k % 2, c["y"] + k + 1)
                        square(k, c["x"] + k + 1)
                    after(n0 + NOUT - 1)
                elif kind == "scores":
                    for h in range(GROUP):
                        act.wait_ge(max_ready, c["h"] + h + 1)
                        head = st["group"] * GROUP + h
                        src = wide[h] if st["layer"] is not None else pr[h]
                        if st["layer"] is None:
                            nc.scalar.activation(esink[:, h, :], nmax[:, h, :], ACT.Exp, bias=sinks[:, head:head + 1])
                        for q in range(TT):
                            e = nc.scalar.activation(pr[h][:, q, :], src[:, q, :], ACT.Exp, bias=nmax[:, h, q:q + 1],
                                                     scale=1.0 if st["layer"] is None else XHD ** -0.5,
                                                     accum_out=den[:, h, q:q + 1])
                        e.then_inc(exp_ready, 1)
                elif kind in ("attend", "swa_attend"):
                    for h in range(GROUP + 1):
                        if h < GROUP:
                            act.wait_ge(pT_done, c["hd"] + h + 1)
                            if c["hd"] + h >= 2:
                                act.wait_ge(pv_done, c["hd"] + h - 1)
                            nc.scalar.activation(prT[h % 2][:, :, :], wide[h][:, :, :], ACT.Copy).then_inc(pT_ready, 1)
                        if kind == "attend" and h >= 1:
                            y_hi(pair(m_hi, h - 1), (h - 1) % 2, c["y"] + h)
                    if kind == "swa_attend":
                        y_hi(pair(m_hi, st["group"]), 0, c["y"] + 1)
                elif kind == "pw1":
                    for k in range(2 * NOUT):
                        if k % 2:
                            act.wait_ge(unit_done, n0 + k + 1)
                            if k > 1:
                                act.wait_ge(glu_ready, c["gl"] + k // 2)
                            for b in range(UB):
                                e = nc.scalar.activation(cv[:, b, :], acc[(n0 + k) % SLOTS][:, b, :], ACT.Sigmoid,
                                                         bias=pc("c_b_pw1", KC + k // 2 * UB + b))
                            e.then_inc(sig_ready, 1)
                        after(n0 + k)
                elif kind == "lnorm":
                    for k in range(NOUT):
                        act.wait_ge(x_ready, c["x"] + k + 1)
                        nc.scalar.activation(squares_of[k][:, :, :], pair(inner, k), ACT.Square).then_inc(sq_ready, 1)
                    rsqrt(c["v"] + 1)
                    for k in range(NOUT):
                        act.wait_ge(conv_ready, c["c"] + k + 1)
                        if k >= 2:
                            act.wait_ge(act_ready, c["a"] + k - 1)
                        for b in range(UB):
                            e = nc.scalar.activation(y[k % 2][:, b, :], inner[:, 2 * k + b, :], ACT.Silu,
                                                     bias=pc("c_ln_b", 2 * k + b))
                        chain.link(e)
                        nc.scalar.activation(pair(m_hi, k), y[k % 2][:, :, :], ACT.Copy).then_inc(yhi_ready, 1)
                elif kind == "ffn":
                    def silu(wait):
                        act.wait_ge(conv_ready, wait)
                        nc.scalar.activation(cv[:, :, :], cv[:, :, :], ACT.Silu).then_inc(silu_ready, 1)

                    def pair_of_units(j):
                        after(n0 - 1, j)
                        silu(j + (c["c"] + 1))
                        after(n0, j)
                        y_hi(z_hi[:, :, :], 0, j + (c["y"] + 1))
                        after(n0 + 1, j)

                    rsqrt(c["v"] + 1)
                    after(n0)
                    silu(c["c"] + 1)
                    y_hi(z_hi[:, :, :], 0, c["y"] + 1)
                    after(n0 + 1)
                    with act.Fori(1, PAIRS - 1) as j:
                        pair_of_units(j)
                    pair_of_units(PAIRS - 1)
                elif kind == "down":
                    for k in range(NOUT):
                        if st["next_g"]:
                            y_hi(pair(h_hi, k), k % 2, c["y"] + k + 1)
                        square(k, c["x"] + k + 1)
                    after(n0)
                elif kind == "final":
                    rsqrt(c["v"] + 1)

        @block.vector
        def _(dve):
            chain = Chain(dve, dve_chain)

            def split_lo(base, i):
                s = base % SLOTS
                dve.wait_ge(hi_ready, i * SLOTS + (base + 1))
                nc.vector.tensor_tensor(wlo[s][:, :, :], raw[s][:, :, :], whi[s][:, :, :].bitcast(F32),
                                        ALU.subtract).then_inc(lo_ready, 1)

            def after(base, i=0):
                if not isinstance(i, int) or base + (i + 1) * SLOTS < N:
                    split_lo(base + SLOTS, i)

            def y_lo(dst, hi, slot, wait):
                dve.wait_ge(yhi_ready, wait)
                nc.vector.tensor_tensor(dst, y[slot][:, :, :], hi.bitcast(F32), ALU.subtract).then_inc(act_ready, 1)

            def y_free(k, c):
                if c["a"] + max(k - 1, 0):
                    dve.wait_ge(act_ready, c["a"] + max(k - 1, 0))

            def sum_squares(k, src, wait):
                dve.wait_ge(sq_ready, wait)
                if k == 0:
                    return
                e = nc.vector.tensor_tensor(ssum[:, :, :], src(k), src(0) if k == 1 else ssum[:, :, :], ALU.add)
                if k == NOUT - 1:
                    e.then_inc(sum_ready, 1)
                else:
                    chain.link(e)

            def squares(k):
                return pair(inner, k)

            def refine(r, v, t, wait):
                dve.wait_ge(r_ready, wait)
                chain.link(nc.vector.tensor_tensor(t, r, r, ALU.mult))
                chain.link(nc.vector.tensor_tensor(t, t, v, ALU.mult))
                chain.link(nc.vector.tensor_scalar(t, t, -0.5, 1.5, ALU.mult, ALU.add))
                chain.link(nc.vector.tensor_tensor(r, r, t, ALU.mult))

            def inverse_rms(stat_wait, c):
                dve.wait_ge(stat_ready, stat_wait)
                nc.vector.tensor_scalar(var[:, :], stat[:, 0, :], 1.0 / D, EPS, ALU.mult, ALU.add).then_inc(var_ready, 1)
                dve.wait_ge(var_ready, c["v"] + 1)
                refine(rs[:, :], var[:, :], nt[:, :], c["r"] + 1)

            def scale_pair(dst, src, key, r0, k):
                for b in range(UB):
                    e = nc.vector.scalar_tensor_tensor(out=dst[:, b, :], in0=src[:, 2 * k + b, :],
                                                       scalar=pc(key, r0 + 2 * k + b), in1=rs[:, :],
                                                       op0=ALU.mult, op1=ALU.mult)
                return e

            def conv3(key, row):
                marks = [None] * UB
                for k in range(TAPS):
                    for b in range(UB):
                        src, w = pad3[:, b, k:k + T], pc(key, row(k, b))
                        if k == 0:
                            e = nc.vector.tensor_scalar(cv[:, b, :], src, w, None, ALU.mult)
                        else:
                            chain.wait(marks[b])
                            e = nc.vector.scalar_tensor_tensor(out=cv[:, b, :], in0=src, scalar=w, in1=cv[:, b, :],
                                                               op0=ALU.mult, op1=ALU.add)
                        if k < TAPS - 1:
                            marks[b] = chain.mark(e)
                return e

            CONV3 = UB * (TAPS - 1)

            def dwconv_part(part):
                j, q = divmod(part, CPARTS)
                marks = [chain.n] * UB
                for k in range(q * CSTEP, min(q * CSTEP + CSTEP, CTAPS)):
                    for b in range(UB):
                        ch = j * UB + b
                        src, w = mid[:, ch, k:k + T], pc("c_w_dw", k * KC + ch)
                        chain.wait(marks[b])
                        if k == 0:
                            e = nc.vector.tensor_scalar(pr[0][:, b, :], src, w, pc("c_b_dw", ch), ALU.mult, ALU.add)
                        else:
                            e = nc.vector.scalar_tensor_tensor(out=inner[:, ch, :] if k == CTAPS - 1 else pr[0][:, b, :],
                                                               in0=src, scalar=w, in1=pr[0][:, b, :],
                                                               op0=ALU.mult, op1=ALU.add)
                        marks[b] = chain.mark(e)

            def next_operand(k, st, c):
                dve.wait_ge(x_ready, c["x"] + k + 1)
                y_free(k, c)
                key, layer = st["next_g"]
                for b in range(UB):
                    e = nc.vector.tensor_scalar(y[k % 2][:, b, :], x[:, 2 * k + b, :], pc(key, layer * KC + 2 * k + b),
                                                None, ALU.mult)
                e.then_inc(y_ready, 1)

            def mem_gain(layer, c):
                for k in range(NOUT):
                    y_free(k, c)
                    for b in range(UB):
                        e = nc.vector.tensor_scalar(y[k % 2][:, b, :], memt[:, 2 * k + b, :],
                                                    pc("norm_mem", layer * KC + 2 * k + b), None, ALU.mult)
                    e.then_inc(y_ready, 1)
                    if k:
                        y_lo(pair(g_lo, k - 1), pair(g_hi, k - 1), (k - 1) % 2, c["a"] + k)
                y_lo(pair(g_lo, NOUT - 1), pair(g_hi, NOUT - 1), (NOUT - 1) % 2, c["a"] + NOUT)

            def take_x(k, bank, bias):
                if bias is None:
                    e = nc.vector.tensor_tensor(pair(x, k), bank[:, :, :], pair(x, k), ALU.add)
                else:
                    for b in range(UB):
                        e = nc.vector.scalar_tensor_tensor(out=x[:, 2 * k + b, :], in0=bank[:, b, :],
                                                           scalar=pc(bias, 2 * k + b), in1=x[:, 2 * k + b, :],
                                                           op0=ALU.add, op1=ALU.add)
                e.then_inc(x_ready, 1)

            def finish_x(k, st, c, unit=None):
                if st["next_g"]:
                    next_operand(k, st, c)
                    if unit is not None and k < NOUT - 1:
                        after(unit)
                    y_lo(pair(h_lo, k), pair(h_hi, k), k % 2, c["a"] + k + 1)
                sum_squares(k, squares, c["x"] + k + 1)
                if unit is not None and k == NOUT - 1:
                    after(unit)

            for st in stages:
                kind, n0, c = st["kind"], st["n0"], st["c"]
                if kind == "start":
                    nc.vector.memset(mid[:, :, 0:PAD], 0.0).then_inc(gate_ready, 1)
                    nc.vector.memset(pad3[:, :, 0:TAPS - 1], 0.0).then_inc(u_ready, 1)

                    def take(dst, src, g, sem):
                        dve.wait_ge(tr_done, g + 1)
                        nc.vector.tensor_copy(dst, src).then_inc(sem, 1)

                    for k in range(NOUT):
                        take(pair(memt, k), wide[k][:, :, :], k, tr_used)
                    take(par[:, 0:4 * P], flat(wide[0]), NOUT, tr_used)
                    take(par[:, 4 * P:nrow], flat(wide[1])[:, 0:nrow - 4 * P], NOUT + 1, tr_used)
                    dve.wait_ge(tr_used, NOUT + 2)
                    mem_gain(0, dict(a=0, y=0))
                    for n in range(SLOTS):
                        split_lo(n, 0)
                    for k in range(NOUT):
                        take(pair(x, k), wide[(6 + k) % 4][:, :, :], 6 + k, x_ready)
                    dve.wait_ge(r_ready, 1)
                    chain.link(nc.vector.tensor_scalar(rstat[:, 3, :], rstat[:, 0, :], 1.0 / D, EPS, ALU.mult, ALU.add))
                    refine(rstat[:, 2, :], rstat[:, 3, :], rstat[:, 4, :], 1)
                    for t in range(TT):
                        e = nc.vector.tensor_scalar(nt[:, t * P:(t + 1) * P], ones[:, :], rstat[:, 2, t:t + 1], None, ALU.mult)
                    e.then_inc(rows_ready, 1)
                    for k in range(NOUT):
                        next_operand(k, st, dict(x=0, a=NOUT))
                        sum_squares(k, squares, k + 1)
                        y_lo(pair(h_lo, k), pair(h_hi, k), k % 2, NOUT + k + 1)
                    take(rs_mem[:, :], wide[2][:, 0, :], 10, rsm_ready)
                elif kind == "mem_scale":
                    mem_gain(st["layer"], c)
                elif kind == "memkv":
                    dve.wait_ge(unit_done, n0 + 1)
                    k, i = st["k"], st["layer"] % 2
                    bank = acc[n0 % SLOTS]
                    if n0 == 0:
                        dve.wait_ge(rsm_ready, 1)
                    if k < NOUT:
                        e = nc.vector.tensor_tensor(pair(memk[i], k), bank[:, :, :], both(rs_mem), ALU.mult)
                    else:
                        for t in range(TT):
                            e = nc.vector.tensor_scalar(memv[i][:, t, (k - NOUT) * UC:(k - NOUT + 1) * UC], bank[:, t, :],
                                                        rstat[:, 2, t:t + 1], None, ALU.mult)
                    e.then_inc(kv_ready, 1)
                    after(n0)
                    if "part" in st:
                        dwconv_part(st["part"])
                elif kind == "norm":
                    inverse_rms(c["st"] + 1, c)
                    key, layer = st["g"]
                    for k in range(NOUT):
                        y_free(k, c)
                        scale_pair(y[k % 2], x, key, layer * KC, k).then_inc(y_ready, 1)
                        if k:
                            y_lo(pair(h_lo, k - 1), pair(h_hi, k - 1), (k - 1) % 2, c["a"] + k)
                    y_lo(pair(h_lo, NOUT - 1), pair(h_hi, NOUT - 1), (NOUT - 1) % 2, c["a"] + NOUT)
                elif kind == "sconv":
                    inverse_rms(c["st"] + 1, c)
                    chain.link(nc.vector.tensor_tensor(nt[:, :], rs[:, :], rs[:, :], ALU.mult))
                    with dve.Fori(0, NOUT) as j:
                        chain.enter(j, CONV3 + 2)
                        dve.wait_ge(unit_done, j * 3 + (n0 + 1))
                        nc.vector.tensor_tensor(y[1][:, :, :], acc[n0 % SLOTS][:, :, :], both(nt),
                                                ALU.mult).then_inc(gate_ready, 1)
                        after(n0, j)
                        dve.wait_ge(gate_ready, j + (c["g"] + 1))
                        dve.wait_ge(unit_done, j * 3 + (n0 + 2))
                        nc.vector.tensor_tensor(pad3[:, :, TAPS - 1:], acc[(n0 + 1) % SLOTS][:, :, :],
                                                y[1][:, :, :], ALU.mult).then_inc(u_ready, 1)
                        dve.wait_ge(u_ready, j + (c["u"] + 1))
                        conv = chain.mark(conv3("a_conv", lambda k, b: j * UB + (st["j"] * TAPS * KC + k * KC + b)))
                        chain.wait(conv)
                        chain.link(nc.vector.tensor_tensor(cv[:, :, :], cv[:, :, :], both(rs), ALU.mult))
                        after(n0 + 1, j)
                        dve.wait_ge(unit_done, j * 3 + (n0 + 3))
                        dve.wait_ge(act_ready, j + c["a"])
                        nc.vector.tensor_tensor(y[0][:, :, :], acc[(n0 + 2) % SLOTS][:, :, :], cv[:, :, :],
                                                ALU.mult).then_inc(y_ready, 1)
                        y_lo(m_lo[:, bass.ds(j * 2, 2), :], m_hi[:, bass.ds(j * 2, 2), :], 0, j + (c["a"] + 1))
                        after(n0 + 2, j)
                    chain.leave(NOUT)
                elif kind == "resid":
                    for k in range(NOUT):
                        dve.wait_ge(unit_done, n0 + k + 1)
                        take_x(k, acc[(n0 + k) % SLOTS], st["bias"])
                        finish_x(k, st, c, n0 + k)
                elif kind == "down":
                    for k in range(NOUT):
                        if k < NOUT - 1:
                            dve.wait_ge(down_ready, c["d"] + k + 1)
                        else:
                            dve.wait_ge(unit_done, n0 + 1)
                        take_x(k, wide[k], None)
                        finish_x(k, st, c)
                    after(n0)
                elif kind == "q":
                    for k in range(NOUT):
                        if k == 0:
                            inverse_rms(c["st"] + 1, c)
                        dve.wait_ge(unit_done, n0 + k + 1)
                        nc.vector.tensor_tensor(pair(inner, k), acc[(n0 + k) % SLOTS][:, :, :], both(rs),
                                                ALU.mult).then_inc(qk_ready, 1)
                        after(n0 + k)
                elif kind == "qkv":
                    for k in range(6):
                        dve.wait_ge(unit_done, n0 + k + 1)
                        bank = acc[(n0 + k) % SLOTS]
                        if k < NOUT:
                            for b in range(UB):
                                e = nc.vector.tensor_scalar(inner[:, 2 * k + b, :], bank[:, b, :], pc("b_b_qkv", 2 * k + b),
                                                            HD ** -0.5, ALU.add, ALU.mult)
                        elif k == NOUT:
                            for b in range(UB):
                                e = nc.vector.tensor_scalar(wk[:, b, :], bank[:, b, :], pc("b_b_qkv", KC + b), None, ALU.add)
                            chain.link(e)
                            nc.vector.tensor_copy(wks[0:HD, :, :], wk[HD:P, :, :])
                            e = nc.vector.tensor_copy(wks[HD:P, :, :], wk[0:HD, :, :])
                        else:
                            dve.wait_ge(bc_landed, 32)
                            for b in range(TT):
                                e = nc.vector.tensor_tensor(wv[:, b, :], bank[:, b, :], vbias, ALU.add)
                        e.then_inc(qk_ready, 1)
                        after(n0 + k)
                elif kind == "scores":
                    def normalise(h):
                        dve.wait_ge(exp_ready, c["h"] + h + 1)
                        if st["layer"] is None:
                            chain.link(nc.vector.tensor_tensor(den[:, h, :], den[:, h, :], esink[:, h, :], ALU.add))
                        chain.link(nc.vector.reciprocal(rden[:, h, :], den[:, h, :]))
                        for q in range(TT):
                            e = nc.vector.tensor_scalar(pr[h][:, q, :], pr[h][:, q, :], rden[:, h, q:q + 1], None, ALU.mult)
                        e.then_inc(prob_ready, 1)

                    for h in range(GROUP):
                        dve.wait_ge(score_done, c["h"] + h + 1)
                        if st["layer"] is None:
                            head = st["group"] * GROUP + h
                            slope = 2.0 ** (-8.0 * (head + 1) / HEADS)
                            chain.link(nc.vector.scalar_tensor_tensor(out=pr[h][:, :, :], in0=dist[:, :, :], scalar=-slope,
                                                                      in1=wide[h][:, :, :], op0=ALU.mult, op1=ALU.add))
                            chain.link(nc.vector.tensor_reduce(rmax[:, h, :], pr[h][:, :, :], AX_X, ALU.max))
                            nc.vector.tensor_scalar(nmax[:, h, :], rmax[:, h, :], sinks[:, head:head + 1], -1.0,
                                                    ALU.max, ALU.mult).then_inc(max_ready, 1)
                        else:
                            chain.link(nc.vector.tensor_reduce(rmax[:, h, :], wide[h][:, :, :], AX_X, ALU.max))
                            nc.vector.tensor_scalar(nmax[:, h, :], rmax[:, h, :], -XHD ** -0.5, None, ALU.mult).then_inc(max_ready, 1)
                        if h:
                            normalise(h - 1)
                    normalise(GROUP - 1)
                elif kind == "attend":
                    for h in range(XH):
                        dve.wait_ge(pv_done, c["hd"] + h + 1)
                        y_free(h, c)
                        nc.vector.tensor_copy(y[h % 2][:, :, :], wide[h][:, :, :]).then_inc(y_ready, 1)
                        if h:
                            y_lo(pair(m_lo, h - 1), pair(m_hi, h - 1), (h - 1) % 2, c["a"] + h)
                    y_lo(pair(m_lo, XH - 1), pair(m_hi, XH - 1), (XH - 1) % 2, c["a"] + XH)
                elif kind == "swa_attend":
                    g = st["group"]
                    dve.wait_ge(pv_done, c["hd"] + GROUP)
                    y_free(0, c)
                    nc.vector.tensor_copy(y[0][:, :, :], wide[0][:, :, :]).then_inc(y_ready, 1)
                    y_lo(pair(m_lo, g), pair(m_hi, g), 0, c["a"] + 1)
                elif kind == "pw1":
                    for k in range(2 * NOUT):
                        if k % 2:
                            j = k // 2
                            dve.wait_ge(unit_done, n0 + k)
                            dve.wait_ge(sig_ready, c["sg"] + j + 1)
                            for b in range(UB):
                                e = nc.vector.scalar_tensor_tensor(out=inner[:, 2 * j + b, :], in0=acc[(n0 + k - 1) % SLOTS][:, b, :],
                                                                   scalar=pc("c_b_pw1", 2 * j + b), in1=cv[:, b, :],
                                                                   op0=ALU.add, op1=ALU.mult)
                            e.then_inc(glu_ready, 1)
                            dve.wait_ge(glu_ready, c["gl"] + j + 1)
                        after(n0 + k)
                        if k:
                            dwconv_part(k - 1)
                elif kind == "lnorm":
                    dwconv_part(st["part"])
                    chain.wait(chain.n)
                    for k in range(1, NOUT):
                        e = nc.vector.tensor_tensor(ssum[:, :, :], pair(inner, k), pair(inner, 0) if k == 1 else ssum[:, :, :],
                                                    ALU.add)
                        if k < NOUT - 1:
                            chain.link(e)
                    e.then_inc(sum_ready, 1)
                    dve.wait_ge(stat_ready, c["st"] + 1)
                    chain.link(nc.vector.tensor_scalar(nt[:, :], stat[:, 0, :], 1.0 / D, None, ALU.mult))
                    for k in range(NOUT):
                        for b in range(UB):
                            e = nc.vector.tensor_tensor(inner[:, 2 * k + b, :], inner[:, 2 * k + b, :], nt[:, :], ALU.subtract)
                        e.then_inc(x_ready, 1)
                    for k in range(NOUT):
                        sum_squares(k, lambda k: squares_of[k][:, :, :], c["x"] + k + 1)
                    inverse_rms(c["st"] + 2, c)
                    for k in range(NOUT):
                        dve.wait_ge(x_ready, c["x"] + NOUT)
                        scale_pair(pair(inner, k), inner, "c_ln_g", 0, k).then_inc(conv_ready, 1)
                        if k:
                            y_lo(pair(m_lo, k - 1), pair(m_hi, k - 1), (k - 1) % 2, c["a"] + k)
                    y_lo(pair(m_lo, NOUT - 1), pair(m_hi, NOUT - 1), (NOUT - 1) % 2, c["a"] + NOUT)
                elif kind == "ffn":
                    def gate_conv(bank, done, wait, j):
                        dve.wait_ge(unit_done, done)
                        nc.vector.tensor_tensor(pad3[:, :, TAPS - 1:], bank[:, :, :], both(rs), ALU.mult).then_inc(gate_ready, 1)
                        dve.wait_ge(gate_ready, wait)
                        conv3("f_conv", lambda k, b: j * UB + ((st["layer"] * TAPS + k) * FC + b)).then_inc(conv_ready, 1)

                    def scale_silu(wait):
                        dve.wait_ge(silu_ready, wait)
                        chain.link(nc.vector.tensor_tensor(cv[:, :, :], cv[:, :, :], both(rs), ALU.mult))

                    def up(wait, waita):
                        dve.wait_ge(unit_done, wait)
                        dve.wait_ge(act_ready, waita - 1)
                        nc.vector.tensor_tensor(y[0][:, :, :], acc[(n0 + 1) % SLOTS][:, :, :], cv[:, :, :],
                                                ALU.mult).then_inc(y_ready, 1)
                        y_lo(z_lo[:, :, :], z_hi[:, :, :], 0, waita)

                    def pair_of_units(j):
                        gate_conv(acc[(n0 - 1) % SLOTS], j * 3 + n0, j + (c["g"] + 1), j)
                        after(n0 - 1, j)
                        scale_silu(j + (c["si"] + 1))
                        after(n0, j)
                        up(j * 3 + (n0 + 2), j + (c["a"] + 1))
                        after(n0 + 1, j)

                    inverse_rms(c["st"] + 1, c)
                    gate_conv(acc[n0 % SLOTS], n0 + 1, c["g"] + 1, 0)
                    after(n0)
                    scale_silu(c["si"] + 1)
                    up(n0 + 2, c["a"] + 1)
                    after(n0 + 1)
                    with dve.Fori(1, PAIRS - 1) as j:
                        chain.enter(j - 1, CONV3 + 1)
                        pair_of_units(j)
                    chain.leave(PAIRS - 2)
                    pair_of_units(PAIRS - 1)
                elif kind == "final":
                    inverse_rms(c["st"] + 1, c)
                    for k in range(NOUT):
                        scale_pair(pair(inner, k), x, "norm_final", 0, k).then_inc(conv_ready, 1)
                    for g in range(2 * TT):
                        t, half = divmod(g, 2)
                        dve.wait_ge(tr_done, c["tr"] + g + 1)
                        nc.vector.tensor_copy(out_rows[:, t, half * 512:(half + 1) * 512],
                                              flat(wide[g])).then_inc(outT_ready, 1)

        @block.tensor
        def _(pe):
            taken = [None] * SLOTS

            def bank_free(n, sem, value):
                if taken[n % SLOTS]:
                    pe.wait_ge(*taken[n % SLOTS])
                taken[n % SLOTS] = (sem, value)

            def products(out_, w, r, first, last):
                pe.matmul(out_, w[0], r[0], start=first, stop=False, skip_group_check=True)
                pe.matmul(out_, w[0], r[1], start=False, stop=False, skip_group_check=True)
                return pe.matmul(out_, w[1], r[0], start=False, stop=last, skip_group_check=True)

            def unit(base, i, operand, ready=None, tokens=False):
                s = base % SLOTS
                pe.wait_ge(lo_ready, i * SLOTS + (base + 1))
                for b in range(UB):
                    for kc in range(KC):
                        if ready is not None and b == 0 and kc % 2 == 0:
                            pe.wait_ge(act_ready, ready[kc // 2])
                        if tokens:
                            e = products(acc[s][:, b, :], [t[:, kc, b * P:(b + 1) * P] for t in operand],
                                         [whi[s][:, kc, :], wlo[s][:, kc, :]], kc == 0, kc == KC - 1)
                        else:
                            e = products(acc[s][:, b, :], [t[s][:, kc, b * P:(b + 1) * P] for t in (whi, wlo)],
                                         [t[:, kc, :] for t in operand], kc == 0, kc == KC - 1)
                e.then_inc(unit_done, 1)

            def down(base, i, ready, first, last):
                s = base % SLOTS
                pe.wait_ge(lo_ready, i * SLOTS + (base + 1))
                pe.wait_ge(act_ready, ready)
                w = [flat(t[s]).rearrange("p (c n) -> p c n", n=D) for t in (whi, wlo)]
                for nb in range(KC):
                    for kc in range(UB):
                        e = products(wide[nb // 2][:, nb % 2, :], [t[:, kc, nb * P:(nb + 1) * P] for t in w],
                                     [t[:, kc, :] for t in (z_hi, z_lo)], first and nb % 2 == 0 and kc == 0,
                                     last and kc == UB - 1)
                    if last and nb % 2 and nb < KC - 1:
                        e.then_inc(down_ready, 1)
                e.then_inc(unit_done, 1)

            def sum_features(wait):
                pe.wait_ge(sum_ready, wait)
                for b in range(UB):
                    e = pe.matmul(stat[:, 0, :], ones[:, :], ssum[:, b, :], start=(b == 0), stop=(b == UB - 1))
                e.then_inc(stat_ready, 1)

            def next_sum():
                su[0] += 1
                sum_features(su[0])

            H, M, G = (h_hi, h_lo), (m_hi, m_lo), (g_hi, g_lo)
            su = [0]
            made = {}
            for st in stages:
                kind, n0, c = st["kind"], st["n0"], st["c"]
                if st.get("next_g"):
                    made["h"] = [c["a"] + k + 1 for k in range(NOUT)]
                if kind == "start":
                    pe.wait_ge(const_ready, CONSTS)

                    def four(bank, srcs):
                        for q, src in enumerate(srcs):
                            e = pe.transpose(bank[:, q // 2, (q % 2) * P:(q % 2 + 1) * P], src, ident[0:src.shape[0], 0:src.shape[0]])
                        e.then_inc(tr_done, 1)

                    def four_each(rows, landed, g0):
                        pe.wait_ge(landed, 16 * TT)
                        for k in range(NOUT):
                            if g0 + k >= 4:
                                pe.wait_ge(tr_used, g0 + k - 3)
                            four(wide[(g0 + k) % 4], [rows[:, t, (2 * k + b) * P:(2 * k + b + 1) * P]
                                                      for b in range(UB) for t in range(TT)])

                    four_each(mem_rows, mem_landed, 0)
                    pe.wait_ge(par_landed, 16 * len(pieces))
                    for q in range(groups):
                        rows = min(P, nrow - q * P)
                        if q % 4 == 0:
                            pe.wait_ge(tr_used, q // 4 + 1)
                        e = pe.transpose(wide[q // 4][:, q % 4 // 2, (q % 2) * P:(q % 2) * P + rows], par_rows[0:rows, q, :],
                                         ident[0:rows, 0:rows])
                        if q in (3, groups - 1):
                            e.then_inc(tr_done, 1)
                    four_each(x_rows, x_landed, 6)
                    made["g"] = [k + 1 for k in range(NOUT)]
                    made["h"] = [NOUT + k + 1 for k in range(NOUT)]
                elif kind == "memkv":
                    k = st["k"]
                    bank_free(n0, kv_ready, c["kv"] + 1)
                    unit(n0, 0, G, ready=made["g"] if k == 0 else None, tokens=k >= NOUT)
                    if n0 == 0:
                        pe.wait_ge(rows_ready, 1)
                        pe.wait_ge(x_ready, 1)
                        for t in range(TT):
                            e = pe.transpose(wide[2][:, 0, t * P:(t + 1) * P], nt[:, t * P:(t + 1) * P], ident[:, :])
                        e.then_inc(tr_done, 1)
                elif kind == "norm":
                    next_sum()
                    made["h"] = [c["a"] + k + 1 for k in range(NOUT)]
                elif kind == "sconv":
                    by = ((gate_ready, c["g"]), (u_ready, c["u"]), (y_ready, c["y"]))
                    next_sum()
                    for u in range(3):
                        bank_free(n0 + u, by[u][0], by[u][1] + NOUT)
                    pe.wait_ge(act_ready, made["h"][-1])
                    with pe.Fori(0, NOUT) as j:
                        for u in range(3):
                            pe.wait_ge(by[u][0], j + by[u][1])
                            unit(n0 + u, j, H)
                    made["m"] = [c["a"] + k + 1 for k in range(NOUT)]
                elif kind in ("resid", "q", "qkv", "pw1"):
                    for k in range(st["units"]):
                        if kind == "resid":
                            bank_free(n0 + k, x_ready, c["x"] + k + 1)
                        elif kind == "pw1":
                            bank_free(n0 + k, *((sig_ready, c["sg"] + k // 2 + 1) if k % 2
                                                else (glu_ready, c["gl"] + k // 2 + 1)))
                        else:
                            bank_free(n0 + k, qk_ready, c["q"] + k + 1)
                        if kind == "resid":
                            unit(n0 + k, 0, M, ready=made["m"] if k == 0 else None)
                        else:
                            unit(n0 + k, 0, H, ready=made["h"] if k == 0 else None, tokens=(kind == "qkv" and k == 5))
                        if kind == "q" and k == 0:
                            next_sum()
                elif kind == "scores":
                    pe.wait_ge(qk_ready, c["q"])
                    if st["layer"] is not None:
                        i = st["layer"] % 2
                        pe.wait_ge(kv_ready, 2 * NOUT * st["layer"] + NOUT)
                    elif st["group"]:
                        pe.wait_ge(y_ready, c["y"])
                    for h in range(GROUP):
                        for q in range(TT):
                            if st["layer"] is not None:
                                for kc in range(UB):
                                    e = pe.matmul(wide[h][:, q, :], inner[:, UB * h + kc, q * P:(q + 1) * P],
                                                  memk[i][:, UB * h + kc, :], start=(kc == 0), stop=(kc == UB - 1))
                            else:
                                head = st["group"] * GROUP + h
                                kv = head // (HEADS // KVH)
                                half = slice(head % 2 * HD, head % 2 * HD + HD)
                                keys = wk if kv % 2 == head % 2 else wks
                                e = pe.matmul(wide[h][:, q, :], inner[half, head // 2, q * P:(q + 1) * P],
                                              keys[half, kv // 2, :], start=True, stop=True)
                        e.then_inc(score_done, 1)
                elif kind in ("attend", "swa_attend"):
                    def transpose_head(h):
                        pe.wait_ge(prob_ready, c["hd"] + h + 1)
                        for kk in range(TT):
                            for q in range(TT):
                                e = pe.transpose(wide[h][:, kk, q * P:(q + 1) * P], pr[h][:, q, kk * P:(kk + 1) * P], ident[:, :])
                        e.then_inc(pT_done, 1)

                    def values(h):
                        pe.wait_ge(pT_ready, c["hd"] + h + 1)
                        if kind == "attend":
                            i = st["layer"] % 2
                            for b in range(UB):
                                for kk in range(TT):
                                    e = pe.matmul(wide[h][:, b, :], memv[i][:, kk, h * XHD + b * P:h * XHD + (b + 1) * P],
                                                  prT[h % 2][:, kk, :], start=(kk == 0), stop=(kk == TT - 1))
                        else:
                            kv = st["group"] * GROUP // (HEADS // KVH)
                            half = slice(h % 2 * HD, h % 2 * HD + HD)
                            for kk in range(TT):
                                e = pe.matmul(wide[0][half, h // 2, :], wv[:, kk, kv * HD:(kv + 1) * HD],
                                              prT[h % 2][:, kk, :], start=(kk == 0), stop=(kk == TT - 1), skip_group_check=True)
                        e.then_inc(pv_done, 1)

                    if kind == "attend":
                        pe.wait_ge(kv_ready, 2 * NOUT * (st["layer"] + 1))
                        made["m"] = [c["a"] + k + 1 for k in range(NOUT)]
                    else:
                        made["m"] = made["m"][:st["group"]] + [c["a"] + 1] if st["group"] else [c["a"] + 1]
                    transpose_head(0)
                    for h in range(1, GROUP):
                        transpose_head(h)
                        values(h - 1)
                    values(GROUP - 1)
                elif kind == "mem_scale":
                    made["g"] = [c["a"] + k + 1 for k in range(NOUT)]
                elif kind == "lnorm":
                    made["m"] = [c["a"] + k + 1 for k in range(NOUT)]
                    for _ in range(2):
                        next_sum()
                elif kind == "ffn":
                    g0, y0, a0 = c["g"], c["y"], c["a"]
                    bank_free(n0, gate_ready, g0 + 1)
                    unit(n0, 0, H, ready=made["h"])
                    next_sum()
                    bank_free(n0 + 1, y_ready, y0 + PAIRS)
                    unit(n0 + 1, 0, H)

                    def pair_of_units(j, first=False):
                        pe.wait_ge(gate_ready, j + g0)
                        unit(n0 - 1, j, H)
                        down(n0, j, j + a0, first, False)
                        pe.wait_ge(y_ready, j + y0)
                        unit(n0 + 1, j, H)

                    bank_free(n0 + 2, gate_ready, g0 + PAIRS)
                    pair_of_units(1, True)
                    with pe.Fori(2, PAIRS) as j:
                        pair_of_units(j)
                    z_ready = a0 + PAIRS
                elif kind == "down":
                    down(n0, 0, z_ready, False, True)
                elif kind == "final":
                    next_sum()
                    for g in range(2 * TT):
                        t, half = divmod(g, 2)
                        pe.wait_ge(conv_ready, c["c"] + 2 * half + 2)
                        for q in range(4):
                            e = pe.transpose(wide[g][:, q // 2, (q % 2) * P:(q % 2 + 1) * P],
                                             inner[:, half * 4 + q, t * P:(t + 1) * P], ident[:, :])
                        e.then_inc(tr_done, 1)


_INS = ["x", "mem", "norm_mix", "norm_xattn", "norm_mem", "norm_ffn", "norm_final",
        "a_w_in", "a_conv", "a_w_out",
        "b_w_qkv", "b_b_qkv", "b_sinks", "b_w_o", "b_b_o",
        "c_w_pw1", "c_b_pw1", "c_w_dw", "c_b_dw", "c_ln_g", "c_ln_b", "c_w_pw2", "c_b_pw2",
        "x_w_q", "x_w_kv", "x_w_o", "f_w_up", "f_conv", "f_w_down"]


def kernel(**inputs):
    import numpy as _np
    import concourse.bacc as _bacc
    from concourse import mybir as _mybir
    from concourse.bass_utils import run_bass_kernel_spmd as _run

    nc = _bacc.Bacc("TRN2", target_bir_lowering=False, num_devices=1)
    arrays, aps = {}, {}
    for name in _INS:
        v = _np.ascontiguousarray(inputs[name])
        arrays[f"in_{name}"] = v
        aps[name] = nc.dram_tensor(f"in_{name}", v.shape, _mybir.dt.from_np(v.dtype), kind="ExternalInput").ap()
    out = nc.dram_tensor("out", (1, T, D), F32, kind="ExternalOutput").ap()
    build(nc, aps, out)
    r = _run(nc, [arrays], core_ids=[0])
    return r.results[0]["out"]
```

```python
from contextlib import ExitStack

import concourse.bass as bass
from concourse import mybir

ALU = mybir.AluOpType
ACT = mybir.ActivationFunctionType
AX_X = mybir.AxisListType.X
F32 = mybir.dt.float32
F32R = mybir.dt.float32r

P = 128
D = 1024
T = 256
DEPTH = 4
KC = D // P
TT = T // P
FF = 2816
FC = FF // P
UC = 256
UB = UC // P
PAIRS = FF // UC
NOUT = D // UC
SLOTS = 3
LAST = SLOTS * (PAIRS - 1)
UBLOCKS = UC * D // (P * P)
TAPS = 3
CTAPS = 31
HEADS = 16
KVH = 4
HD = 64
XH = 4
XHD = D // XH
PAD = CTAPS - 1
CPARTS = 4
PW_PAIRS = (3, 0, 1, 2)
DW = 4
CSTEP = -(-CTAPS // CPARTS)
GROUP = 4
EPS = 1e-6
FAR = 1e30

ADDS = {
    "start": dict(x=4, r=1, tr=11, g=1, u=1, a=4, y=4),
    "x_in": dict(su=1),
    "mem_scale": dict(a=4, y=4),
    "memk": dict(kv=1),
    "memv": dict(mv=1),
    "sconv": dict(a=4, y=4, g=4, u=4, st=1, v=1, r=1),
    "resid": dict(x=4, su=1),
    "q": dict(q=4, st=1, v=1, r=1),
    "qkv": dict(q=6, st=1, v=1, r=1, tr=1),
    "scores": dict(h=GROUP),
    "attend": dict(a=XH, y=XH, hd=GROUP),
    "swa": dict(a=1, y=1, hd=GROUP, h=GROUP),
    "swa_last": dict(a=1, y=1, hd=GROUP),
    "pw1": dict(sg=4, gl=4, u=4, g=4, st=1, v=1, r=1),
    "dwconv": dict(),
    "ln_mean": dict(su=1, st=1),
    "ln_var": dict(x=4, su=1, st=1),
    "ln_out": dict(a=4, v=1, r=1, c=4),
    "ffn": dict(st=1, v=1, r=1, a=PAIRS, y=PAIRS, g=PAIRS, c=PAIRS, si=PAIRS),
    "down": dict(x=4, su=1, d=3),
    "final": dict(st=1, v=1, r=1, c=4, tr=4),
}


class Chain:

    def __init__(self, eng, sem):
        self.eng, self.sem, self.n, self.i, self.per = eng, sem, 0, 0, 0

    def mark(self, ins):
        self.n += 1
        ins.then_inc(self.sem, 1)
        return self.n

    def wait(self, mark):
        self.eng.wait_ge(self.sem, mark if self.per == 0 else self.i * self.per + mark)

    def link(self, ins):
        self.wait(self.mark(ins))

    def enter(self, i, per):
        self.i, self.per, self.start = i, per, self.n

    def leave(self, trips):
        assert self.n - self.start == self.per, (self.n - self.start, self.per)
        self.n = self.start + trips * self.per
        self.i = self.per = 0


def build(nc, a, out):
    params = [
        ("norm_mem", a["norm_mem"].rearrange("i (c p) -> (i c) p", p=P)),
        ("norm_mix", a["norm_mix"].rearrange("i (c p) -> (i c) p", p=P)),
        ("norm_xattn", a["norm_xattn"].rearrange("i (c p) -> (i c) p", p=P)),
        ("norm_ffn", a["norm_ffn"].rearrange("i (c p) -> (i c) p", p=P)),
        ("a_conv", a["a_conv"].rearrange("j k (c p) -> (j k c) p", p=P)),
        ("norm_final", a["norm_final"].rearrange("(c p) -> c p", p=P)),
        ("b_b_qkv", a["b_b_qkv"].rearrange("j (c p) -> (j c) p", p=P)),
        ("b_b_o", a["b_b_o"].rearrange("j (c p) -> (j c) p", p=P)),
        ("c_b_pw1", a["c_b_pw1"].rearrange("j (c p) -> (j c) p", p=P)),
        ("c_b_dw", a["c_b_dw"].rearrange("j (c p) -> (j c) p", p=P)),
        ("c_ln_g", a["c_ln_g"].rearrange("j (c p) -> (j c) p", p=P)),
        ("c_ln_b", a["c_ln_b"].rearrange("j (c p) -> (j c) p", p=P)),
        ("c_b_pw2", a["c_b_pw2"].rearrange("j (c p) -> (j c) p", p=P)),
        ("f_conv", a["f_conv"].rearrange("i k (c p) -> (i k c) p", p=P)),
        ("c_w_dw", a["c_w_dw"].rearrange("j k (c p) -> (j k c) p", p=P)),
    ]
    col, nrow = {}, 0
    for key, ap in params:
        col[key] = nrow
        nrow += ap.shape[0]
    groups = -(-nrow // P)
    pieces = []
    for key, ap in params:
        r = 0
        while r < ap.shape[0]:
            g, p0 = divmod(col[key] + r, P)
            k = min(ap.shape[0] - r, P - p0)
            pieces.append((g, p0, k, ap[r:r + k, :]))
            r += k

    stages = []
    counts = dict(n=0)

    def stage(kind, units=0, **kw):
        stages.append(dict(kind=kind, n0=counts["n"], units=units, c=dict(counts), **kw))
        counts["n"] += units
        for key, v in ADDS[kind].items():
            counts[key] = counts.get(key, 0) + v
        if kw.get("next_g") or kw.get("scale_for"):
            counts["a"] += NOUT
            counts["y"] += NOUT

    for adds in ADDS.values():
        for key in adds:
            counts.setdefault(key, 0)
    filled = [0]

    def fill(count):
        for _ in range(count):
            layer, k = divmod(filled[0], 2 * NOUT)
            stage("memk" if k < NOUT else "memv", 1, layer=layer, k=k)
            filled[0] += 1

    def split_later():
        stages[-1]["late"] = True
        return stages[-1]["n0"]

    def mem_scale(layer):
        assert filled[0] == 2 * NOUT * layer
        stage("mem_scale", layer=layer)

    def shortconv(layer, j):
        stages[-1]["sum_next"] = True
        stage("sconv", 3 * NOUT, j=j)
        fill(1)
        stage("resid", NOUT, w=a["a_w_out"][j], bias=None, next_g=("norm_xattn", layer))

    def xattn(layer, f_softmax, scale_for=None, early=None):
        stage("q", NOUT, layer=layer, scale_for=early)
        stage("scores", layer=layer, group=0)
        fill(f_softmax)
        stage("attend", layer=layer, group=0, late=split_later())
        if scale_for:
            mem_scale(scale_for)
        stage("resid", NOUT, w=a["x_w_o"][layer], bias=None, next_g=("norm_ffn", layer))

    def ffn(layer, f_norm, next_g=None):
        stage("ffn", 3 * PAIRS - 1, layer=layer)
        stage("down", 1, layer=layer, next_g=next_g)
        fill(f_norm)

    stage("start")
    fill(2)
    stage("x_in", next_g=("norm_mix", 0))
    fill(3)
    shortconv(0, 0)
    xattn(0, 2, scale_for=1)
    ffn(0, 2, next_g=("norm_mix", 1))
    stage("qkv", 6)
    stage("scores", layer=None, group=0)
    for group in range(HEADS // GROUP):
        fill(1)
        stage("swa" if group < HEADS // GROUP - 1 else "swa_last", layer=None, group=group,
              late=split_later())
    stage("resid", NOUT, w=a["b_w_o"][0], bias="b_b_o", next_g=("norm_xattn", 1))
    xattn(1, 2, scale_for=2)
    ffn(1, 2, next_g=("norm_mix", 2))
    stage("pw1", 2 * NOUT)
    stage("dwconv", i=0, parts=[2, 3])
    fill(1)
    stage("dwconv", i=1, parts=[4, 5])
    stage("dwconv", i=2, parts=[6])
    stage("dwconv", i=3, parts=[7])
    stage("ln_mean")
    fill(1)
    stage("ln_var")
    fill(2)
    stage("ln_out")
    fill(2)
    stage("resid", NOUT, w=a["c_w_pw2"][0], bias="c_b_pw2", next_g=("norm_xattn", 2))
    xattn(2, 2, early=3)
    ffn(2, 3, next_g=("norm_mix", 3))
    shortconv(3, 1)
    xattn(3, 2)
    ffn(3, 0)
    stage("final")
    assert filled[0] == 2 * NOUT * DEPTH
    N = counts["n"]

    with ExitStack() as ctx:
        def sb(name, shape, dt=F32):
            return ctx.enter_context(nc.sbuf_tensor(name, shape, dt))

        def ps(name, shape):
            return ctx.enter_context(nc.psum_tensor(name, shape, F32))

        def sem(name):
            return ctx.enter_context(nc.semaphore(name))

        raw = [sb(f"raw{s}", [P, KC, UC]) for s in range(SLOTS)]
        whi = [sb(f"whi{s}", [P, KC, UC], F32R) for s in range(SLOTS)]
        wlo = [sb(f"wlo{s}", [P, KC, UC], F32R) for s in range(SLOTS)]
        x = sb("x", [P, KC, T])
        h_hi, h_lo = sb("h_hi", [P, KC, T], F32R), sb("h_lo", [P, KC, T], F32R)
        m_hi, m_lo = sb("m_hi", [P, KC, T], F32R), sb("m_lo", [P, KC, T], F32R)
        z_hi, z_lo = sb("z_hi", [P, UB, T], F32R), sb("z_lo", [P, UB, T], F32R)
        memt = sb("memt", [P, KC, T])
        g_hi, g_lo = sb("g_hi", [P, KC, T], F32R), sb("g_lo", [P, KC, T], F32R)
        memk = [sb(f"memk{i}", [P, KC, T]) for i in range(2)]
        memv = [sb(f"memv{i}", [P, TT, D]) for i in range(2)]
        mid = sb("mid", [P, KC, PAD + T])
        inner = mid[:, :, PAD:PAD + T]
        pad3 = sb("pad3", [P, UB, TAPS - 1 + T])
        cv = sb("cv", [P, UB, T])
        y = [sb(f"y{i}", [P, UB, T]) for i in range(2)]
        ssum = sb("ssum", [P, UB, T])
        rs, var, nt = sb("rs", [P, T]), sb("var", [P, T]), sb("nt", [P, T])
        rs_mem = sb("rs_mem", [P, T])
        par = sb("par", [P, groups * P])
        ident, ones = sb("ident", [P, P]), sb("ones", [P, P])
        eps_c = sb("eps_c", [P, 1])
        dist = sb("dist", [P, TT, T])
        sinks = sb("sinks", [P, HEADS])
        pr = [sb(f"pr{i}", [P, TT, T]) for i in range(GROUP - 1)] + [ssum]
        prT = [cv, pad3[:, :, TAPS - 1:]]
        squares_of = pr[0:3] + [cv]
        rmax, nmax = sb("rmax", [P, GROUP, TT]), sb("nmax", [P, GROUP, TT])
        den, esink, rden = (sb(k, [P, GROUP, TT]) for k in ("den", "esink", "rden"))
        rstat = sb("rstat", [P, 6, TT])

        def both(t):
            return t[:, :].unsqueeze(1).broadcast_to([P, UB, T])

        def flat(t):
            return t[:, :, :].rearrange("p a b -> p (a b)")

        dw_chunks = [KC - 2, KC - 1, KC - 4, KC - 3]
        assert len(dw_chunks) == DW

        half_taps = [range(0, UBLOCKS), range(UBLOCKS, CTAPS)]

        def diag(half, k):
            return flat((memk[1], memv[1])[half])[:, k % UBLOCKS * P:(k % UBLOCKS + 1) * P]
        x_rows = flat(memk[1]).rearrange("p (t d) -> p t d", t=TT)
        mem_rows = memv[1]
        par_rows = flat(memk[0])[:, 0:groups * P].rearrange("p (g c) -> p g c", c=P)
        out_rows = memv[0]
        wk, wks = memk[0][:, 0:2, :], memk[0][:, 2:4, :]
        wv, vbias = memk[0][:, 4:6, :], memk[0][:, 6, :]

        acc = [ps(f"acc{i}", [P, UB, T]) for i in range(SLOTS)]
        wide = [ps(f"wide{i}", [P, UB, T]) for i in range(NOUT)]
        stat = ps("stat", [P, UB, T])

        out_banks = acc + wide[0:1]
        w_landed = [sem(f"w_landed{s}") for s in range(SLOTS)]
        hi_ready = sem("hi_ready")
        lo_ready = sem("lo_ready")
        unit_done = sem("unit_done")
        u_ready = sem("u_ready")
        glu_ready = sem("glu_ready")
        diag_ready = sem("diag_ready")
        dw_done = sem("dw_done")
        par_landed, x_landed, mem_landed = sem("par_landed"), sem("x_landed"), sem("mem_landed")
        bc_landed = sem("bc_landed")
        const_ready = sem("const_ready")
        rows_ready = sem("rows_ready")
        rsm_ready = sem("rsm_ready")
        tr_done = sem("tr_done")
        tr_used = sem("tr_used")
        x_ready = sem("x_ready")
        sq_ready = sem("sq_ready")
        sum_ready = sem("sum_ready")
        stat_ready = sem("stat_ready")
        var_ready = sem("var_ready")
        r_ready = sem("r_ready")
        y_ready = sem("y_ready")
        yhi_ready = sem("yhi_ready")
        act_ready = sem("act_ready")
        gate_ready = sem("gate_ready")
        sig_ready = sem("sig_ready")
        conv_ready = sem("conv_ready")
        silu_ready = sem("silu_ready")
        down_ready = sem("down_ready")
        qk_ready = sem("qk_ready")
        kv_ready = sem("kv_ready")
        v_ready = sem("v_ready")
        score_done = sem("score_done")
        max_ready = sem("max_ready")
        exp_ready = sem("exp_ready")
        prob_ready = sem("prob_ready")
        pT_done = sem("pT_done")
        pT_ready = sem("pT_ready")
        pv_done = sem("pv_done")
        outT_ready = sem("outT_ready")
        stored = sem("stored")
        dve_chain, act_chain, pool_chain = sem("dve_chain"), sem("act_chain"), sem("pool_chain")

        def pc(key, r, parts=slice(None)):
            return par[parts, bass.ds(r + col[key], 1)]

        def pair(t, k):
            return t[:, 2 * k:2 * k + 2, :]

        block = ctx.enter_context(nc.Block())

        @block.sync
        def _(sp):
            def load(base, i, src):
                s = base % SLOTS
                if not isinstance(i, int) or base >= SLOTS:
                    sp.wait_ge(lo_ready, i * SLOTS + (base - SLOTS + 1))
                dst = raw[s][:, :, :] if src.shape[1] == KC else flat(raw[s]).rearrange("p (c n) -> p c n", n=D)
                sp.dma_start(dst, src).then_inc(w_landed[s], 16)

            def wcols(w, c0):
                return w[:, bass.ds(c0, UC)].rearrange("(c p) n -> p c n", p=P)

            def wrows(w, r0):
                return w[bass.ds(r0, UC), :].rearrange("(c p) n -> p c n", p=P)

            for st in stages:
                kind, n0 = st["kind"], st["n0"]
                if kind == "start":
                    for t in range(TT):
                        sp.dma_start(mem_rows[:, t, :], a["mem"][0, t * P:(t + 1) * P, :]).then_inc(mem_landed, 16)
                    load(0, 0, wcols(a["x_w_kv"][0], 0))
                    for g, p0, k, src in pieces[::2]:
                        sp.dma_start(par_rows[p0:p0 + k, g, :], src).then_inc(par_landed, 16)
                    for t in range(TT):
                        sp.dma_start(x_rows[:, t, :], a["x"][0, t * P:(t + 1) * P, :]).then_inc(x_landed, 16)
                    sp.wait_ge(par_landed, 16 * len(pieces))
                elif kind in ("memk", "memv") and n0:
                    load(n0, 0, wcols(a["x_w_kv"][st["layer"]], st["k"] * UC))
                elif kind == "sconv":
                    w = a["a_w_in"][st["j"]]
                    with sp.Fori(1, NOUT + 1) as j1:
                        for u, part in enumerate((1, 2, 0)):
                            load(n0 + u - SLOTS, j1, wcols(w, j1 * UC + (part * D - UC)))
                elif kind in ("resid", "q"):
                    w = st["w"] if kind == "resid" else a["x_w_q"][st["layer"]]
                    for k in range(NOUT):
                        load(n0 + k, 0, wcols(w, k * UC))
                elif kind == "qkv":
                    for k in range(6):
                        load(n0 + k, 0, wcols(a["b_w_qkv"][0], k * UC))
                elif kind == "pw1":
                    for k in range(2 * NOUT):
                        load(n0 + k, 0, wcols(a["c_w_pw1"][0], (k % 2) * D + PW_PAIRS[k // 2] * UC))
                elif kind == "ffn":
                    w_up, w_down = a["f_w_up"][st["layer"]], a["f_w_down"][st["layer"]]
                    load(n0, 0, wcols(w_up, 0))
                    load(n0 + 1, 0, wcols(w_up, FF))
                    with sp.Fori(2, PAIRS) as j1:
                        load(n0 - 1 - SLOTS, j1, wcols(w_up, j1 * UC + (-UC)))
                        load(n0 - SLOTS, j1, wrows(w_down, j1 * UC + (-2 * UC)))
                        load(n0 + 1 - SLOTS, j1, wcols(w_up, j1 * UC + (FF - UC)))
                    load(n0 + LAST - 1, 0, wcols(w_up, (PAIRS - 1) * UC))
                    load(n0 + LAST, 0, wcols(w_up, FF + (PAIRS - 1) * UC))
                    load(n0 + LAST + 1, 0, wrows(w_down, (PAIRS - 2) * UC))
                elif kind == "down":
                    load(n0, 0, wrows(a["f_w_down"][st["layer"]], (PAIRS - 1) * UC))
            for g in range(2 * TT):
                t, half = divmod(g, 2)
                sp.wait_ge(outT_ready, g + 1)
                sp.dma_start(out[0, t * P:(t + 1) * P, half * 512:(half + 1) * 512],
                             out_rows[:, t, half * 512:(half + 1) * 512]).then_inc(stored, 16)
            sp.wait_ge(stored, 16 * 2 * TT)

        @block.gpsimd
        def _(pool):
            pool.dma_start(sinks[:, :], a["b_sinks"][0].partition_broadcast(P)).then_inc(bc_landed, 16)
            chain = Chain(pool, pool_chain)
            pool.memset(ones[:, :], 1.0).then_inc(const_ready, 1)
            pool.memset(eps_c[:, :], EPS).then_inc(const_ready, 1)
            chain.link(pool.memset(ident[:, :], 0.0))
            pool.affine_select(out=ident[:, :], in_=ident[:, :], compare_op=ALU.not_equal, fill=1.0, base=0,
                               pattern=[[-1, P]], channel_multiplier=1).then_inc(const_ready, 1)
            chain.link(pool.iota(dist[:, :, :], [[P, TT], [-1, T]], base=0, channel_multiplier=1,
                                 allow_small_or_imprecise_dtypes=True))
            chain.link(pool.affine_select(out=dist[:, :, :], in_=dist[:, :, :], compare_op=ALU.is_ge, fill=FAR,
                                          base=0, pattern=[[P, TT], [-1, T]], channel_multiplier=1))
            pool.affine_select(out=dist[:, :, :], in_=dist[:, :, :], compare_op=ALU.is_ge, fill=FAR,
                               base=P - 1, pattern=[[-P, TT], [1, T]], channel_multiplier=-1).then_inc(const_ready, 1)
            pool.wait_ge(pv_done, XH)
            pool.dma_start(vbias, a["b_b_qkv"][0, (HEADS + KVH) * HD:].partition_broadcast(P)).then_inc(bc_landed, 16)

        CONSTS = 4

        @block.scalar
        def _(act):
            chain = Chain(act, act_chain)

            def split_hi(base, i):
                s = base % SLOTS
                act.wait_ge(w_landed[s], i * 16 + 16 * (base // SLOTS + 1))
                if base >= SLOTS:
                    act.wait_ge(unit_done, i * SLOTS + (base - SLOTS + 1))
                nc.scalar.activation(whi[s][:, :, :], raw[s][:, :, :], ACT.Copy).then_inc(hi_ready, 1)

            def after(base, i=0):
                if not isinstance(i, int) or base + (i + 1) * SLOTS < N:
                    split_hi(base + SLOTS, i)

            def y_hi(dst, slot, wait):
                act.wait_ge(y_ready, wait)
                nc.scalar.activation(dst, y[slot][:, :, :], ACT.Copy).then_inc(yhi_ready, 1)

            def square(k, wait):
                act.wait_ge(x_ready, wait)
                nc.scalar.activation(pair(inner, k), pair(x, k), ACT.Square).then_inc(sq_ready, 1)

            def rsqrt(wait):
                act.wait_ge(var_ready, wait)
                chain.link(nc.scalar.activation(nt[:, :], var[:, :], ACT.Ln))
                nc.scalar.activation(rs[:, :], nt[:, :], ACT.Exp, scale=-0.5).then_inc(r_ready, 1)

            def exponentials(layer, group, h, c):
                act.wait_ge(max_ready, c["h"] + h + 1)
                head = group * GROUP + h
                src = wide[h] if layer is not None else pr[h]
                if layer is None:
                    nc.scalar.activation(esink[:, h, :], nmax[:, h, :], ACT.Exp, bias=sinks[:, head:head + 1])
                for q in range(TT):
                    e = nc.scalar.activation(pr[h][:, q, :], src[:, q, :], ACT.Exp, bias=nmax[:, h, q:q + 1],
                                             scale=1.0 if layer is None else XHD ** -0.5, accum_out=den[:, h, q:q + 1])
                e.then_inc(exp_ready, 1)

            def transposed(h, c):
                act.wait_ge(pT_done, c["hd"] + h + 1)
                if c["hd"] + h >= 2:
                    act.wait_ge(pv_done, c["hd"] + h - 1)
                nc.scalar.activation(prT[h % 2][:, :, :], wide[h][:, :, :], ACT.Copy).then_inc(pT_ready, 1)

            for st in stages:
                kind, n0, c = st["kind"], st["n0"], st["c"]
                if kind == "start":
                    for g, p0, k, src in pieces[1::2]:
                        act.dma_start(par_rows[p0:p0 + k, g, :], src).then_inc(par_landed, 16)
                    act.wait_ge(const_ready, CONSTS)
                    act.wait_ge(mem_landed, 16 * TT)
                    for t in range(TT):
                        e = nc.scalar.activation(memv[0][:, t, :], mem_rows[:, t, :], ACT.Square,
                                                 accum_out=rstat[:, 0, t:t + 1])
                    chain.link(e)
                    chain.link(nc.scalar.activation(rstat[:, 1, :], rstat[:, 0, :], ACT.Ln, bias=eps_c[:, 0:1],
                                                    scale=1.0 / D))
                    nc.scalar.activation(rstat[:, 2, :], rstat[:, 1, :], ACT.Exp, scale=-0.5).then_inc(r_ready, 1)
                    split_hi(0, 0)
                    for k in range(NOUT):
                        y_hi(pair(g_hi, k), k % 2, k + 1)
                    for n in range(1, SLOTS):
                        split_hi(n, 0)
                elif kind == "x_in":
                    for k in range(NOUT):
                        square(k, k + 1)
                        y_hi(pair(h_hi, k), k % 2, c["y"] + k + 1)
                elif kind == "mem_scale":
                    for k in range(NOUT):
                        y_hi(pair(g_hi, k), k % 2, c["y"] + k + 1)
                elif kind in ("memk", "memv", "q", "qkv"):
                    for k in range(st["units"]):
                        if kind in ("q", "qkv") and k == 0:
                            rsqrt(c["v"] + 1)
                        if kind == "memv":
                            act.wait_ge(unit_done, n0 + 1)
                            i, c0 = st["layer"] % 2, (st["k"] - NOUT) * UC
                            for t in range(TT):
                                e = nc.scalar.activation(memv[i][:, t, c0:c0 + UC], acc[n0 % SLOTS][:, t, :], ACT.Copy,
                                                         scale=rstat[:, 2, t:t + 1])
                            e.then_inc(v_ready, 1)
                        if not st.get("late"):
                            after(n0 + k)
                        if st.get("scale_for"):
                            y_hi(pair(g_hi, k), k % 2, c["y"] + k + 1)
                elif kind == "sconv":
                    rsqrt(c["v"] + 1)
                    with act.Fori(0, NOUT) as j:
                        after(n0, j)
                        after(n0 + 1, j)
                        y_hi(m_hi[:, bass.ds(j * 2, 2), :], 0, j + (c["y"] + 1))
                        after(n0 + 2, j)
                elif kind == "resid":
                    for k in range(NOUT):
                        if k < NOUT - 1:
                            after(n0 + k)
                        y_hi(pair(h_hi, k), k % 2, c["y"] + k + 1)
                        square(k, c["x"] + k + 1)
                    after(n0 + NOUT - 1)
                elif kind == "scores":
                    for h in range(GROUP):
                        exponentials(st["layer"], st["group"], h, c)
                elif kind == "attend":
                    for h in range(GROUP + 1):
                        if h < GROUP:
                            transposed(h, c)
                        if h == 1:
                            after(st["late"])
                        if h >= 1:
                            y_hi(pair(m_hi, h - 1), (h - 1) % 2, c["y"] + h)
                elif kind == "swa":
                    for h in range(3):
                        transposed(h, c)
                    after(st["late"])
                    exponentials(None, st["group"] + 1, 0, c)
                    transposed(3, c)
                    exponentials(None, st["group"] + 1, 1, c)
                    y_hi(pair(m_hi, st["group"]), 0, c["y"] + 1)
                    exponentials(None, st["group"] + 1, 2, c)
                    exponentials(None, st["group"] + 1, 3, c)
                elif kind == "swa_last":
                    for h in range(GROUP):
                        transposed(h, c)
                        if h == 1:
                            after(st["late"])
                    y_hi(pair(m_hi, st["group"]), 0, c["y"] + 1)
                elif kind == "dwconv":
                    if st["i"] + 1 < DW:
                        for half in range(2):
                            act.wait_ge(dw_done, 2 * st["i"] + half + 1)
                            diagonals(st["i"] + 1, half, half_taps[half])
                elif kind == "pw1":
                    def diagonals(i, half, taps):
                        for k in taps:
                            e = nc.scalar.activation(diag(half, k), ident[:, :], ACT.Copy,
                                                     scale=pc("c_w_dw", k * KC + dw_chunks[i]))
                        if k == half_taps[half][-1]:
                            e.then_inc(diag_ready, 1)

                    for k in range(2 * NOUT):
                        if k == 0:
                            rsqrt(c["v"] + 1)
                        if k % 2:
                            act.wait_ge(gate_ready, c["g"] + k // 2 + 1)
                            for b in range(UB):
                                e = nc.scalar.activation(cv[:, b, :], cv[:, b, :], ACT.Sigmoid,
                                                         bias=pc("c_b_pw1", KC + PW_PAIRS[k // 2] * UB + b))
                            e.then_inc(sig_ready, 1)
                        after(n0 + k)
                        if k % 2 == 0:
                            half, part = divmod(k // 2, 2)
                            taps = half_taps[half]
                            diagonals(0, half, taps[:len(taps) // 2] if part == 0 else taps[len(taps) // 2:])
                elif kind == "ln_var":
                    for k in range(NOUT):
                        act.wait_ge(x_ready, c["x"] + k + 1)
                        nc.scalar.activation(squares_of[k][:, :, :], pair(inner, k), ACT.Square).then_inc(sq_ready, 1)
                elif kind == "ln_out":
                    rsqrt(c["v"] + 1)
                    for k in range(NOUT):
                        act.wait_ge(conv_ready, c["c"] + k + 1)
                        if k >= 2:
                            act.wait_ge(act_ready, c["a"] + k - 1)
                        for b in range(UB):
                            e = nc.scalar.activation(y[k % 2][:, b, :], inner[:, 2 * k + b, :], ACT.Silu,
                                                     bias=pc("c_ln_b", 2 * k + b))
                        chain.link(e)
                        nc.scalar.activation(pair(m_hi, k), y[k % 2][:, :, :], ACT.Copy).then_inc(yhi_ready, 1)
                elif kind == "ffn":
                    def silu(wait):
                        act.wait_ge(conv_ready, wait)
                        nc.scalar.activation(cv[:, :, :], cv[:, :, :], ACT.Silu).then_inc(silu_ready, 1)

                    def pair_of_units(j):
                        after(n0 - 1, j)
                        silu(j + (c["c"] + 1))
                        after(n0, j)
                        y_hi(z_hi[:, :, :], 0, j + (c["y"] + 1))
                        after(n0 + 1, j)

                    rsqrt(c["v"] + 1)
                    after(n0)
                    silu(c["c"] + 1)
                    y_hi(z_hi[:, :, :], 0, c["y"] + 1)
                    after(n0 + 1)
                    with act.Fori(1, PAIRS - 1) as j:
                        pair_of_units(j)
                    after(n0 + LAST - 1)
                    silu(c["c"] + PAIRS)
                    y_hi(pair(m_hi, 0), 0, c["y"] + PAIRS)
                    after(n0 + LAST)
                    after(n0 + LAST + 1)
                elif kind == "down":
                    for k in range(NOUT):
                        if st["next_g"]:
                            y_hi(pair(h_hi, k), k % 2, c["y"] + k + 1)
                        square(k, c["x"] + k + 1)
                        if k == 2:
                            after(n0)
                elif kind == "final":
                    act.wait_ge(var_ready, c["v"] + 1)
                    chain.link(nc.scalar.activation(rstat[:, 1, :], rstat[:, 3, :], ACT.Ln))
                    nc.scalar.activation(rstat[:, 2, :], rstat[:, 1, :], ACT.Exp, scale=-0.5).then_inc(r_ready, 1)

        @block.vector
        def _(dve):
            chain = Chain(dve, dve_chain)

            def split_lo(base, i):
                s = base % SLOTS
                dve.wait_ge(hi_ready, i * SLOTS + (base + 1))
                nc.vector.tensor_tensor(wlo[s][:, :, :], raw[s][:, :, :], whi[s][:, :, :].bitcast(F32),
                                        ALU.subtract).then_inc(lo_ready, 1)

            def after(base, i=0):
                if not isinstance(i, int) or base + (i + 1) * SLOTS < N:
                    split_lo(base + SLOTS, i)

            def y_lo(dst, hi, slot, wait):
                dve.wait_ge(yhi_ready, wait)
                nc.vector.tensor_tensor(dst, y[slot][:, :, :], hi.bitcast(F32), ALU.subtract).then_inc(act_ready, 1)

            def y_free(k, c):
                if c["a"] + max(k - 1, 0):
                    dve.wait_ge(act_ready, c["a"] + max(k - 1, 0))

            def sum_squares(k, src, wait):
                dve.wait_ge(sq_ready, wait)
                if k == 0:
                    return
                e = nc.vector.tensor_tensor(ssum[:, :, :], src(k), src(0) if k == 1 else ssum[:, :, :], ALU.add)
                if k == NOUT - 1:
                    e.then_inc(sum_ready, 1)
                else:
                    chain.link(e)

            def squares(k):
                return pair(inner, k)

            def refine(r, v, t, wait):
                dve.wait_ge(r_ready, wait)
                chain.link(nc.vector.tensor_tensor(t, r, r, ALU.mult))
                chain.link(nc.vector.tensor_tensor(t, t, v, ALU.mult))
                chain.link(nc.vector.tensor_scalar(t, t, -0.5, 1.5, ALU.mult, ALU.add))
                chain.link(nc.vector.tensor_tensor(r, r, t, ALU.mult))

            def inverse_rms(stat_wait, c):
                dve.wait_ge(stat_ready, stat_wait)
                nc.vector.tensor_scalar(var[:, :], stat[:, 0, :], 1.0 / D, EPS, ALU.mult, ALU.add).then_inc(var_ready, 1)
                dve.wait_ge(var_ready, c["v"] + 1)
                refine(rs[:, :], var[:, :], nt[:, :], c["r"] + 1)

            def scale_pair(dst, src, key, r0, k):
                for b in range(UB):
                    e = nc.vector.scalar_tensor_tensor(out=dst[:, b, :], in0=src[:, 2 * k + b, :],
                                                       scalar=pc(key, r0 + 2 * k + b), in1=rs[:, :],
                                                       op0=ALU.mult, op1=ALU.mult)
                return e

            def conv3(key, row):
                marks = [None] * UB
                for k in range(TAPS):
                    for b in range(UB):
                        src, w = pad3[:, b, k:k + T], pc(key, row(k, b))
                        if k == 0:
                            e = nc.vector.tensor_scalar(cv[:, b, :], src, w, None, ALU.mult)
                        else:
                            chain.wait(marks[b])
                            e = nc.vector.scalar_tensor_tensor(out=cv[:, b, :], in0=src, scalar=w, in1=cv[:, b, :],
                                                               op0=ALU.mult, op1=ALU.add)
                        if k < TAPS - 1:
                            marks[b] = chain.mark(e)
                return e

            CONV3 = UB * (TAPS - 1)

            def dwconv_part(part):
                j, q = divmod(part, CPARTS)
                marks = [chain.n] * UB
                for k in range(q * CSTEP, min(q * CSTEP + CSTEP, CTAPS)):
                    for b in range(UB):
                        ch = j * UB + b
                        src, w = mid[:, ch, k:k + T], pc("c_w_dw", k * KC + ch)
                        chain.wait(marks[b])
                        if k == 0:
                            e = nc.vector.tensor_scalar(pr[0][:, b, :], src, w, pc("c_b_dw", ch), ALU.mult, ALU.add)
                        else:
                            e = nc.vector.scalar_tensor_tensor(out=inner[:, ch, :] if k == CTAPS - 1 else pr[0][:, b, :],
                                                               in0=src, scalar=w, in1=pr[0][:, b, :],
                                                               op0=ALU.mult, op1=ALU.add)
                        marks[b] = chain.mark(e)

            def next_operand(k, st, c):
                dve.wait_ge(x_ready, c["x"] + k + 1)
                y_free(k, c)
                key, layer = st["next_g"]
                for b in range(UB):
                    e = nc.vector.tensor_scalar(y[k % 2][:, b, :], x[:, 2 * k + b, :], pc(key, layer * KC + 2 * k + b),
                                                None, ALU.mult)
                e.then_inc(y_ready, 1)

            def mem_gain_pair(layer, c, k):
                if k < NOUT:
                    y_free(k, c)
                    for b in range(UB):
                        e = nc.vector.tensor_scalar(y[k % 2][:, b, :], memt[:, 2 * k + b, :],
                                                    pc("norm_mem", layer * KC + 2 * k + b), None, ALU.mult)
                    e.then_inc(y_ready, 1)
                if k:
                    y_lo(pair(g_lo, k - 1), pair(g_hi, k - 1), (k - 1) % 2, c["a"] + k)

            def mem_gain(layer, c):
                for k in range(NOUT + 1):
                    mem_gain_pair(layer, c, k)

            def take_x(k, bank, bias):
                if bias is None:
                    e = nc.vector.tensor_tensor(pair(x, k), bank[:, :, :], pair(x, k), ALU.add)
                else:
                    for b in range(UB):
                        e = nc.vector.scalar_tensor_tensor(out=x[:, 2 * k + b, :], in0=bank[:, b, :],
                                                           scalar=pc(bias, 2 * k + b), in1=x[:, 2 * k + b, :],
                                                           op0=ALU.add, op1=ALU.add)
                e.then_inc(x_ready, 1)

            def finish_x(k, st, c, unit):
                next_operand(k, st, c)
                if k < NOUT - 1:
                    after(unit)
                y_lo(pair(h_lo, k), pair(h_hi, k), k % 2, c["a"] + k + 1)
                sum_squares(k, squares, c["x"] + k + 1)
                if k == NOUT - 1:
                    after(unit)

            def maximum(layer, group, h, c):
                dve.wait_ge(score_done, c["h"] + h + 1)
                if layer is None:
                    head = group * GROUP + h
                    slope = 2.0 ** (-8.0 * (head + 1) / HEADS)
                    chain.link(nc.vector.scalar_tensor_tensor(out=pr[h][:, :, :], in0=dist[:, :, :], scalar=-slope,
                                                              in1=wide[h][:, :, :], op0=ALU.mult, op1=ALU.add))
                    chain.link(nc.vector.tensor_reduce(rmax[:, h, :], pr[h][:, :, :], AX_X, ALU.max))
                    nc.vector.tensor_scalar(nmax[:, h, :], rmax[:, h, :], sinks[:, head:head + 1], -1.0,
                                            ALU.max, ALU.mult).then_inc(max_ready, 1)
                else:
                    chain.link(nc.vector.tensor_reduce(rmax[:, h, :], wide[h][:, :, :], AX_X, ALU.max))
                    nc.vector.tensor_scalar(nmax[:, h, :], rmax[:, h, :], -XHD ** -0.5, None, ALU.mult).then_inc(max_ready, 1)

            def normalise(layer, h, c):
                dve.wait_ge(exp_ready, c["h"] + h + 1)
                if layer is None:
                    chain.link(nc.vector.tensor_tensor(den[:, h, :], den[:, h, :], esink[:, h, :], ALU.add))
                chain.link(nc.vector.reciprocal(rden[:, h, :], den[:, h, :]))
                for q in range(TT):
                    e = nc.vector.tensor_scalar(pr[h][:, q, :], pr[h][:, q, :], rden[:, h, q:q + 1], None, ALU.mult)
                e.then_inc(prob_ready, 1)

            for st in stages:
                kind, n0, c = st["kind"], st["n0"], st["c"]
                if kind == "start":
                    nc.vector.memset(mid[:, :, 0:PAD], 0.0).then_inc(gate_ready, 1)
                    nc.vector.memset(pad3[:, :, 0:TAPS - 1], 0.0).then_inc(u_ready, 1)

                    def take(dst, src, g, sem):
                        dve.wait_ge(tr_done, g + 1)
                        nc.vector.tensor_copy(dst, src).then_inc(sem, 1)

                    for k in range(NOUT):
                        take(pair(memt, k), wide[k][:, :, :], k, tr_used)
                    dve.wait_ge(r_ready, 1)
                    chain.link(nc.vector.tensor_scalar(rstat[:, 3, :], rstat[:, 0, :], 1.0 / D, EPS, ALU.mult, ALU.add))
                    refine(rstat[:, 2, :], rstat[:, 3, :], rstat[:, 4, :], 1)
                    for t in range(TT):
                        e = nc.vector.tensor_scalar(nt[:, t * P:(t + 1) * P], ones[:, :], rstat[:, 2, t:t + 1], None, ALU.mult)
                    e.then_inc(rows_ready, 1)
                    take(par[:, 0:4 * P], flat(wide[0]), NOUT, tr_used)
                    take(par[:, 4 * P:nrow], flat(wide[1])[:, 0:nrow - 4 * P], NOUT + 1, tr_used)
                    split_lo(0, 0)
                    dve.wait_ge(tr_used, NOUT + 2)
                    mem_gain(0, dict(a=0, y=0))
                    take(rs_mem[:, :], stat[:, 0, :], 10, rsm_ready)
                    split_lo(1, 0)
                    for k in range(NOUT):
                        take(pair(x, k), wide[(6 + k) % 4][:, :, :], 6 + k, x_ready)
                    split_lo(2, 0)
                elif kind == "x_in":
                    for k in range(NOUT):
                        next_operand(k, st, dict(x=0, a=c["a"]))
                        if k:
                            y_lo(pair(h_lo, k - 1), pair(h_hi, k - 1), (k - 1) % 2, c["a"] + k)
                        sum_squares(k, squares, k + 1)
                    y_lo(pair(h_lo, NOUT - 1), pair(h_hi, NOUT - 1), (NOUT - 1) % 2, c["a"] + NOUT)
                elif kind == "mem_scale":
                    mem_gain(st["layer"], c)
                elif kind == "memk":
                    if n0 == 0:
                        dve.wait_ge(rsm_ready, 1)
                    dve.wait_ge(unit_done, n0 + 1)
                    nc.vector.tensor_tensor(pair(memk[st["layer"] % 2], st["k"]), acc[n0 % SLOTS][:, :, :], both(rs_mem),
                                            ALU.mult).then_inc(kv_ready, 1)
                    if not st.get("late"):
                        after(n0)
                elif kind == "memv":
                    if not st.get("late"):
                        after(n0)
                elif kind == "sconv":
                    inverse_rms(c["st"] + 1, c)
                    chain.link(nc.vector.tensor_tensor(nt[:, :], rs[:, :], rs[:, :], ALU.mult))
                    with dve.Fori(0, NOUT) as j:
                        chain.enter(j, CONV3 + 2)
                        dve.wait_ge(unit_done, j * 3 + (n0 + 1))
                        nc.vector.tensor_tensor(y[1][:, :, :], acc[n0 % SLOTS][:, :, :], both(nt),
                                                ALU.mult).then_inc(gate_ready, 1)
                        after(n0, j)
                        dve.wait_ge(gate_ready, j + (c["g"] + 1))
                        dve.wait_ge(unit_done, j * 3 + (n0 + 2))
                        nc.vector.tensor_tensor(pad3[:, :, TAPS - 1:], acc[(n0 + 1) % SLOTS][:, :, :],
                                                y[1][:, :, :], ALU.mult).then_inc(u_ready, 1)
                        dve.wait_ge(u_ready, j + (c["u"] + 1))
                        conv = chain.mark(conv3("a_conv", lambda k, b: j * UB + (st["j"] * TAPS * KC + k * KC + b)))
                        chain.wait(conv)
                        chain.link(nc.vector.tensor_tensor(cv[:, :, :], cv[:, :, :], both(rs), ALU.mult))
                        after(n0 + 1, j)
                        dve.wait_ge(unit_done, j * 3 + (n0 + 3))
                        dve.wait_ge(act_ready, j + c["a"])
                        nc.vector.tensor_tensor(y[0][:, :, :], acc[(n0 + 2) % SLOTS][:, :, :], cv[:, :, :],
                                                ALU.mult).then_inc(y_ready, 1)
                        y_lo(m_lo[:, bass.ds(j * 2, 2), :], m_hi[:, bass.ds(j * 2, 2), :], 0, j + (c["a"] + 1))
                        after(n0 + 2, j)
                    chain.leave(NOUT)
                elif kind == "resid":
                    for k in range(NOUT):
                        dve.wait_ge(unit_done, n0 + k + 1)
                        take_x(k, acc[(n0 + k) % SLOTS], st["bias"])
                        finish_x(k, st, c, n0 + k)
                elif kind == "down":
                    def complete(k):
                        if st["next_g"]:
                            y_lo(pair(h_lo, k), pair(h_hi, k), k % 2, c["a"] + k + 1)
                        sum_squares(k, squares, c["x"] + k + 1)

                    for k in range(NOUT):
                        if k < NOUT - 1:
                            dve.wait_ge(down_ready, c["d"] + k + 1)
                        else:
                            dve.wait_ge(unit_done, n0 + 1)
                        take_x(k, wide[k], None)
                        if st["next_g"]:
                            next_operand(k, st, c)
                        else:
                            dve.wait_ge(x_ready, c["x"] + k + 1)
                            for b in range(UB):
                                e = nc.vector.tensor_scalar(memt[:, 2 * k + b, :], x[:, 2 * k + b, :],
                                                            pc("norm_final", 2 * k + b), None, ALU.mult)
                            e.then_inc(conv_ready, 1)
                        if k:
                            complete(k - 1)
                        if k == 2:
                            after(n0)
                    complete(NOUT - 1)
                elif kind == "q":
                    for k in range(NOUT):
                        if k == 0:
                            inverse_rms(c["st"] + 1, c)
                        dve.wait_ge(unit_done, n0 + k + 1)
                        nc.vector.tensor_tensor(pair(inner, k), acc[(n0 + k) % SLOTS][:, :, :], both(rs),
                                                ALU.mult).then_inc(qk_ready, 1)
                        if st["scale_for"]:
                            mem_gain_pair(st["scale_for"], c, k)
                        after(n0 + k)
                    if st["scale_for"]:
                        mem_gain_pair(st["scale_for"], c, NOUT)
                elif kind == "qkv":
                    for k in range(6):
                        if k == 0:
                            inverse_rms(c["st"] + 1, c)
                            nc.vector.tensor_copy(nt[:, :], rs[:, :]).then_inc(rows_ready, 1)
                        dve.wait_ge(unit_done, n0 + k + 1)
                        bank = acc[(n0 + k) % SLOTS]
                        if k < NOUT:
                            chain.link(nc.vector.tensor_tensor(pair(inner, k), bank[:, :, :], both(rs), ALU.mult))
                            for b in range(UB):
                                e = nc.vector.tensor_scalar(inner[:, 2 * k + b, :], inner[:, 2 * k + b, :],
                                                            pc("b_b_qkv", 2 * k + b), HD ** -0.5, ALU.add, ALU.mult)
                        elif k == NOUT:
                            chain.link(nc.vector.tensor_tensor(wk, bank[:, :, :], both(rs), ALU.mult))
                            for b in range(UB):
                                e = nc.vector.tensor_scalar(wk[:, b, :], wk[:, b, :], pc("b_b_qkv", KC + b), None, ALU.add)
                            chain.link(e)
                            nc.vector.tensor_copy(wks[0:HD, :, :], wk[HD:P, :, :])
                            e = nc.vector.tensor_copy(wks[HD:P, :, :], wk[0:HD, :, :])
                        else:
                            dve.wait_ge(tr_done, c["tr"] + 1)
                            for t in range(TT):
                                e = nc.vector.tensor_copy(rstat[:, 5, t:t + 1], stat[:, 1, t * P:t * P + 1])
                            chain.link(e)
                            dve.wait_ge(bc_landed, 32)
                            for t in range(TT):
                                e = nc.vector.scalar_tensor_tensor(out=wv[:, t, :], in0=bank[:, t, :], scalar=rstat[:, 5, t:t + 1],
                                                                   in1=vbias, op0=ALU.mult, op1=ALU.add)
                        e.then_inc(qk_ready, 1)
                        after(n0 + k)
                elif kind == "scores":
                    for h in range(GROUP):
                        maximum(st["layer"], st["group"], h, c)
                        if h:
                            normalise(st["layer"], h - 1, c)
                    normalise(st["layer"], GROUP - 1, c)
                elif kind == "attend":
                    for h in range(XH):
                        dve.wait_ge(pv_done, c["hd"] + h + 1)
                        y_free(h, c)
                        nc.vector.tensor_copy(y[h % 2][:, :, :], wide[h][:, :, :]).then_inc(y_ready, 1)
                        if h == 0:
                            after(st["late"])
                        if h:
                            y_lo(pair(m_lo, h - 1), pair(m_hi, h - 1), (h - 1) % 2, c["a"] + h)
                    y_lo(pair(m_lo, XH - 1), pair(m_hi, XH - 1), (XH - 1) % 2, c["a"] + XH)
                elif kind in ("swa", "swa_last"):
                    def take_heads():
                        dve.wait_ge(pv_done, c["hd"] + GROUP)
                        y_free(0, c)
                        nc.vector.tensor_copy(y[0][:, :, :], stat[:, :, :]).then_inc(y_ready, 1)

                    def split_heads():
                        y_lo(pair(m_lo, g), pair(m_hi, g), 0, c["a"] + 1)

                    g = st["group"]
                    if kind == "swa":
                        maximum(None, g + 1, 0, c)
                        maximum(None, g + 1, 1, c)
                        after(st["late"])
                        normalise(None, 0, c)
                        maximum(None, g + 1, 2, c)
                        normalise(None, 1, c)
                        take_heads()
                        maximum(None, g + 1, 3, c)
                        normalise(None, 2, c)
                        split_heads()
                        normalise(None, 3, c)
                    else:
                        take_heads()
                        after(st["late"])
                        split_heads()
                elif kind == "pw1":
                    for k in range(2 * NOUT):
                        j = k // 2
                        if k == 0:
                            inverse_rms(c["st"] + 1, c)
                        dve.wait_ge(unit_done, n0 + k + 1)
                        bank = acc[(n0 + k) % SLOTS]
                        if k % 2 == 0:
                            nc.vector.tensor_tensor(pad3[:, :, TAPS - 1:], bank[:, :, :], both(rs), ALU.mult).then_inc(u_ready, 1)
                        else:
                            nc.vector.tensor_tensor(cv[:, :, :], bank[:, :, :], both(rs), ALU.mult).then_inc(gate_ready, 1)
                            dve.wait_ge(u_ready, c["u"] + j + 1)
                            dve.wait_ge(sig_ready, c["sg"] + j + 1)
                            for b in range(UB):
                                ch = UB * PW_PAIRS[j] + b
                                e = nc.vector.scalar_tensor_tensor(out=inner[:, ch, :], in0=pad3[:, b, TAPS - 1:],
                                                                   scalar=pc("c_b_pw1", ch), in1=cv[:, b, :],
                                                                   op0=ALU.add, op1=ALU.mult)
                            e.then_inc(glu_ready, 1)
                            dve.wait_ge(glu_ready, c["gl"] + j + 1)
                        after(n0 + k)
                        if k in (4, 5):
                            dwconv_part((4, 5).index(k))
                elif kind == "dwconv":
                    for part in st["parts"]:
                        dwconv_part(part)
                elif kind == "ln_mean":
                    for i, ch in enumerate(dw_chunks):
                        dve.wait_ge(dw_done, 2 * i + 2)
                        e = nc.vector.tensor_scalar(inner[:, ch, :], wide[i][:, 0, :], pc("c_b_dw", ch), None, ALU.add)
                    chain.link(e)
                    for k in range(1, NOUT):
                        e = nc.vector.tensor_tensor(ssum[:, :, :], pair(inner, k), pair(inner, 0) if k == 1 else ssum[:, :, :],
                                                    ALU.add)
                        if k < NOUT - 1:
                            chain.link(e)
                    e.then_inc(sum_ready, 1)
                elif kind == "ln_var":
                    dve.wait_ge(stat_ready, c["st"])
                    chain.link(nc.vector.tensor_scalar(nt[:, :], stat[:, 0, :], 1.0 / D, None, ALU.mult))
                    for k in range(NOUT):
                        for b in range(UB):
                            e = nc.vector.tensor_tensor(inner[:, 2 * k + b, :], inner[:, 2 * k + b, :], nt[:, :], ALU.subtract)
                        e.then_inc(x_ready, 1)
                    for k in range(NOUT):
                        sum_squares(k, lambda k: squares_of[k][:, :, :], c["x"] + k + 1)
                elif kind == "ln_out":
                    inverse_rms(c["st"], c)
                    for k in range(NOUT):
                        dve.wait_ge(x_ready, c["x"])
                        scale_pair(pair(inner, k), inner, "c_ln_g", 0, k).then_inc(conv_ready, 1)
                        if k >= 2:
                            y_lo(pair(m_lo, k - 2), pair(m_hi, k - 2), k % 2, c["a"] + k - 1)
                    for k in range(NOUT - 2, NOUT):
                        y_lo(pair(m_lo, k), pair(m_hi, k), k % 2, c["a"] + k + 1)
                elif kind == "ffn":
                    def gate_conv(bank, done, wait, j):
                        dve.wait_ge(unit_done, done)
                        nc.vector.tensor_tensor(pad3[:, :, TAPS - 1:], bank[:, :, :], both(rs), ALU.mult).then_inc(gate_ready, 1)
                        dve.wait_ge(gate_ready, wait)
                        conv3("f_conv", lambda k, b: j * UB + ((st["layer"] * TAPS + k) * FC + b)).then_inc(conv_ready, 1)

                    def scale_silu(wait):
                        dve.wait_ge(silu_ready, wait)
                        chain.link(nc.vector.tensor_tensor(cv[:, :, :], cv[:, :, :], both(rs), ALU.mult))

                    def up(bank, wait, waita, lo, hi):
                        dve.wait_ge(unit_done, wait)
                        dve.wait_ge(act_ready, waita - 1)
                        nc.vector.tensor_tensor(y[0][:, :, :], bank[:, :, :], cv[:, :, :], ALU.mult).then_inc(y_ready, 1)
                        y_lo(lo, hi, 0, waita)

                    def pair_of_units(j):
                        gate_conv(acc[(n0 - 1) % SLOTS], j * 3 + n0, j + (c["g"] + 1), j)
                        after(n0 - 1, j)
                        scale_silu(j + (c["si"] + 1))
                        after(n0, j)
                        up(acc[(n0 + 1) % SLOTS], j * 3 + (n0 + 2), j + (c["a"] + 1), z_lo[:, :, :], z_hi[:, :, :])
                        after(n0 + 1, j)

                    inverse_rms(c["st"] + 1, c)
                    gate_conv(acc[n0 % SLOTS], n0 + 1, c["g"] + 1, 0)
                    after(n0)
                    scale_silu(c["si"] + 1)
                    up(acc[(n0 + 1) % SLOTS], n0 + 2, c["a"] + 1, z_lo[:, :, :], z_hi[:, :, :])
                    after(n0 + 1)
                    with dve.Fori(1, PAIRS - 1) as j:
                        chain.enter(j - 1, CONV3 + 1)
                        pair_of_units(j)
                    chain.leave(PAIRS - 2)
                    gate_conv(acc[(n0 - 1) % SLOTS], n0 + LAST, c["g"] + PAIRS, PAIRS - 1)
                    after(n0 + LAST - 1)
                    scale_silu(c["si"] + PAIRS)
                    up(acc[n0 % SLOTS], n0 + LAST + 1, c["a"] + PAIRS, pair(m_lo, 0), pair(m_hi, 0))
                    after(n0 + LAST)
                    after(n0 + LAST + 1)
                elif kind == "final":
                    dve.wait_ge(stat_ready, c["st"] + 1)
                    nc.vector.tensor_scalar(rstat[:, 3, :], stat[:, :, 0], 1.0 / D, EPS, ALU.mult, ALU.add).then_inc(var_ready, 1)
                    dve.wait_ge(var_ready, c["v"] + 1)
                    refine(rstat[:, 2, :], rstat[:, 3, :], rstat[:, 4, :], c["r"] + 1)
                    for g in range(2 * TT):
                        t, half = divmod(g, 2)
                        dve.wait_ge(tr_done, c["tr"] + half * TT + t + 1)
                        nc.vector.tensor_scalar(out_rows[:, t, half * 512:(half + 1) * 512], flat(out_banks[half * TT + t]),
                                                rstat[:, 2, t:t + 1], None, ALU.mult).then_inc(outT_ready, 1)

        @block.tensor
        def _(pe):
            taken = [None] * SLOTS

            def bank_free(n, sem, value):
                if taken[n % SLOTS]:
                    pe.wait_ge(*taken[n % SLOTS])
                taken[n % SLOTS] = (sem, value)

            def products(out_, w, r, first, last):
                pe.matmul(out_, w[0], r[0], start=first, stop=False, skip_group_check=True)
                pe.matmul(out_, w[0], r[1], start=False, stop=False, skip_group_check=True)
                return pe.matmul(out_, w[1], r[0], start=False, stop=last, skip_group_check=True)

            def unit(base, i, operand, ready=None, tokens=False, between=None):
                s = base % SLOTS
                pe.wait_ge(lo_ready, i * SLOTS + (base + 1))
                if ready is None:
                    order = [(b, kc) for b in range(UB) for kc in range(KC)]
                else:
                    order = [(b, kc) for last in range(2) for b in range(UB) for kc in range(KC) if (kc >= KC - 2) == last]
                for q, (b, kc) in enumerate(order):
                    if between and q == len(order) - 2 * UB:
                        between()
                    if ready is not None and kc % 2 == 0 and kc not in [o[1] for o in order[:q]]:
                        pe.wait_ge(act_ready, ready[kc // 2])
                    first, final = q == 0, q == len(order) - 1
                    if tokens:
                        e = products(acc[s][:, b, :], [t[:, kc, b * P:(b + 1) * P] for t in operand],
                                     [whi[s][:, kc, :], wlo[s][:, kc, :]], first, final)
                    else:
                        e = products(acc[s][:, b, :], [t[s][:, kc, b * P:(b + 1) * P] for t in (whi, wlo)],
                                     [t[:, kc, :] for t in operand], first, final)
                e.then_inc(unit_done, 1)

            def down(base, i, ready, first, last, operand):
                s = base % SLOTS
                pe.wait_ge(lo_ready, i * SLOTS + (base + 1))
                pe.wait_ge(act_ready, ready)
                w = [flat(t[s]).rearrange("p (c n) -> p c n", n=D) for t in (whi, wlo)]
                for nb in range(KC):
                    for kc in range(UB):
                        e = products(wide[nb // 2][:, nb % 2, :], [t[:, kc, nb * P:(nb + 1) * P] for t in w],
                                     [t[:, kc, :] for t in operand], first and nb % 2 == 0 and kc == 0,
                                     last and kc == UB - 1)
                    if last and nb % 2 and nb < KC - 1:
                        e.then_inc(down_ready, 1)
                e.then_inc(unit_done, 1)

            def sum_features(wait):
                pe.wait_ge(sum_ready, wait)
                for b in range(UB):
                    e = pe.matmul(stat[:, 0, :], ones[:, :], ssum[:, b, :], start=(b == 0), stop=(b == UB - 1))
                e.then_inc(stat_ready, 1)

            def next_sum():
                su[0] += 1
                sum_features(su[0])

            def scores(layer, group, h):
                for q in range(TT):
                    if layer is not None:
                        for kc in range(UB):
                            e = pe.matmul(wide[h][:, q, :], inner[:, UB * h + kc, q * P:(q + 1) * P],
                                          memk[layer % 2][:, UB * h + kc, :], start=(kc == 0), stop=(kc == UB - 1))
                    else:
                        head = group * GROUP + h
                        kv = head // (HEADS // KVH)
                        half = slice(head % 2 * HD, head % 2 * HD + HD)
                        keys = wk if kv % 2 == head % 2 else wks
                        e = pe.matmul(wide[h][:, q, :], inner[half, head // 2, q * P:(q + 1) * P],
                                      keys[half, kv // 2, :], start=True, stop=True)
                e.then_inc(score_done, 1)

            def transpose_head(h, c):
                pe.wait_ge(prob_ready, c["hd"] + h + 1)
                for kk in range(TT):
                    for q in range(TT):
                        e = pe.transpose(wide[h][:, kk, q * P:(q + 1) * P], pr[h][:, q, kk * P:(kk + 1) * P], ident[:, :])
                e.then_inc(pT_done, 1)

            def values(st, h, c):
                pe.wait_ge(pT_ready, c["hd"] + h + 1)
                if st["kind"] == "attend":
                    i = st["layer"] % 2
                    for b in range(UB):
                        for kk in range(TT):
                            e = pe.matmul(wide[h][:, b, :], memv[i][:, kk, h * XHD + b * P:h * XHD + (b + 1) * P],
                                          prT[h % 2][:, kk, :], start=(kk == 0), stop=(kk == TT - 1))
                else:
                    kv = st["group"] * GROUP // (HEADS // KVH)
                    half = slice(h % 2 * HD, h % 2 * HD + HD)
                    for kk in range(TT):
                        e = pe.matmul(stat[half, h // 2, :], wv[:, kk, kv * HD:(kv + 1) * HD],
                                      prT[h % 2][:, kk, :], start=(kk == 0), stop=(kk == TT - 1), skip_group_check=True)
                e.then_inc(pv_done, 1)

            H, M, G = (h_hi, h_lo), (m_hi, m_lo), (g_hi, g_lo)
            su = [0]
            sum_due = [0]
            made = {}
            for st in stages:
                kind, n0, c = st["kind"], st["n0"], st["c"]
                if st.get("next_g"):
                    made["h"] = [c["a"] + k + 1 for k in range(NOUT)]
                if st.get("scale_for"):
                    made["g"] = [c["a"] + k + 1 for k in range(NOUT)]
                if kind == "start":
                    pe.wait_ge(const_ready, CONSTS)

                    def four(bank, srcs):
                        for q, src in enumerate(srcs):
                            e = pe.transpose(bank[:, q // 2, (q % 2) * P:(q % 2 + 1) * P], src, ident[0:src.shape[0], 0:src.shape[0]])
                        e.then_inc(tr_done, 1)

                    def four_each(rows, landed, g0):
                        pe.wait_ge(landed, 16 * TT)
                        for k in range(NOUT):
                            if g0 + k >= 4:
                                pe.wait_ge(tr_used, g0 + k - 3)
                            four(wide[(g0 + k) % 4], [rows[:, t, (2 * k + b) * P:(2 * k + b + 1) * P]
                                                      for b in range(UB) for t in range(TT)])

                    four_each(mem_rows, mem_landed, 0)
                    pe.wait_ge(par_landed, 16 * len(pieces))
                    for q in range(groups):
                        rows = min(P, nrow - q * P)
                        if q % 4 == 0:
                            pe.wait_ge(tr_used, q // 4 + 1)
                        e = pe.transpose(wide[q // 4][:, q % 4 // 2, (q % 2) * P:(q % 2) * P + rows], par_rows[0:rows, q, :],
                                         ident[0:rows, 0:rows])
                        if q in (3, groups - 1):
                            e.then_inc(tr_done, 1)
                    four_each(x_rows, x_landed, 6)
                    pe.wait_ge(rows_ready, 1)
                    for t in range(TT):
                        e = pe.transpose(stat[:, 0, t * P:(t + 1) * P], nt[:, t * P:(t + 1) * P], ident[:, :])
                    e.then_inc(tr_done, 1)
                    made["g"] = [k + 1 for k in range(NOUT)]
                elif kind in ("memk", "memv"):
                    k = st["k"]
                    bank_free(n0, *((kv_ready, c["kv"] + 1) if kind == "memk" else (v_ready, c["mv"] + 1)))
                    unit(n0, 0, G, ready=made["g"] if k == 0 else None, tokens=k >= NOUT)
                    if sum_due[0] == 1 or st.get("sum_next"):
                        next_sum()
                    sum_due[0] = max(sum_due[0] - 1, 0)
                elif kind == "sconv":
                    by = ((gate_ready, c["g"]), (u_ready, c["u"]), (y_ready, c["y"]))
                    for u in range(3):
                        bank_free(n0 + u, by[u][0], by[u][1] + NOUT)
                    pe.wait_ge(act_ready, made["h"][-1])
                    with pe.Fori(0, NOUT) as j:
                        for u in range(3):
                            pe.wait_ge(by[u][0], j + by[u][1])
                            unit(n0 + u, j, H)
                    made["m"] = [c["a"] + k + 1 for k in range(NOUT)]
                elif kind in ("resid", "q", "qkv", "pw1"):
                    for k in range(st["units"]):
                        if kind == "resid":
                            bank_free(n0 + k, x_ready, c["x"] + k + 1)
                        elif kind == "pw1":
                            bank_free(n0 + k, *((gate_ready, c["g"] + k // 2 + 1) if k % 2
                                                else (u_ready, c["u"] + k // 2 + 1)))
                        else:
                            bank_free(n0 + k, qk_ready, c["q"] + k + 1)
                        if kind == "resid":
                            unit(n0 + k, 0, M, ready=made["m"] if k == 0 else None)
                        else:
                            unit(n0 + k, 0, H, ready=made["h"] if k == 0 else None, tokens=(kind == "qkv" and k == 5),
                                 between=next_sum if k == 0 else None)
                        if kind == "qkv" and k == 1:
                            pe.wait_ge(rows_ready, 2)
                            for t in range(TT):
                                e = pe.transpose(stat[:, 1, t * P:(t + 1) * P], nt[:, t * P:(t + 1) * P], ident[:, :])
                            e.then_inc(tr_done, 1)
                elif kind == "scores":
                    if st["layer"] is not None:
                        pe.wait_ge(kv_ready, NOUT * (st["layer"] + 1))
                    else:
                        pe.wait_ge(qk_ready, c["q"] - 1)
                    for h in range(GROUP):
                        if st["layer"] is not None:
                            pe.wait_ge(qk_ready, c["q"] - GROUP + h + 1)
                        scores(st["layer"], st["group"], h)
                elif kind == "attend":
                    made["m"] = [c["a"] + k + 1 for k in range(NOUT)]
                    for h in range(GROUP + 2):
                        if h < GROUP:
                            transpose_head(h, c)
                        if h == 2:
                            pe.wait_ge(v_ready, NOUT * (st["layer"] + 1))
                        if h >= 2:
                            values(st, h - 2, c)
                elif kind in ("swa", "swa_last"):
                    made["m"] = (made["m"] if st["group"] else []) + [c["a"] + 1]
                    transpose_head(0, c)
                    for h in range(1, GROUP + 1):
                        if h < GROUP:
                            transpose_head(h, c)
                        if h == 1 and st["group"]:
                            pe.wait_ge(y_ready, c["y"])
                        values(st, h - 1, c)
                        if kind == "swa":
                            scores(None, st["group"] + 1, h - 1)
                elif kind == "mem_scale":
                    made["g"] = [c["a"] + k + 1 for k in range(NOUT)]
                elif kind == "dwconv":
                    i = st["i"]
                    pe.wait_ge(glu_ready, c["gl"] - (NOUT - 1 if i < UB else 0))
                    for half in range(2):
                        pe.wait_ge(diag_ready, 2 * i + half + 1)
                        for k in half_taps[half]:
                            e = pe.matmul(wide[i][:, 0, :], diag(half, k), mid[:, dw_chunks[i], k:k + T],
                                          start=(k == 0), stop=(k == CTAPS - 1))
                        e.then_inc(dw_done, 1)
                elif kind in ("ln_mean", "ln_var"):
                    sum_due[0] = 1 if kind == "ln_mean" else 2
                elif kind == "ln_out":
                    made["m"] = [c["a"] + k + 1 for k in range(NOUT)]
                elif kind == "ffn":
                    g0, y0, a0 = c["g"], c["y"], c["a"]
                    bank_free(n0, gate_ready, g0 + 1)
                    unit(n0, 0, H, ready=made["h"], between=next_sum)
                    bank_free(n0 + 1, y_ready, y0 + PAIRS - 1)
                    unit(n0 + 1, 0, H)

                    def pair_of_units(j, first=False):
                        pe.wait_ge(gate_ready, j + g0)
                        unit(n0 - 1, j, H)
                        down(n0, j, j + a0, first, False, (z_hi, z_lo))
                        pe.wait_ge(y_ready, j + y0)
                        unit(n0 + 1, j, H)

                    bank_free(n0 + 2, gate_ready, g0 + PAIRS)
                    pair_of_units(1, True)
                    with pe.Fori(2, PAIRS - 1) as j:
                        pair_of_units(j)
                    pe.wait_ge(gate_ready, g0 + PAIRS - 1)
                    unit(n0 + LAST - 1, 0, H)
                    unit(n0 + LAST, 0, H)
                    down(n0 + LAST + 1, 0, a0 + PAIRS - 1, False, False, (z_hi, z_lo))
                    taken[n0 % SLOTS] = (y_ready, y0 + PAIRS)
                    z_ready = a0 + PAIRS
                elif kind == "down":
                    down(n0, 0, z_ready, False, True, M)
                elif kind == "final":
                    for half in range(2):
                        pe.wait_ge(conv_ready, c["c"] + 2 * half + 2)
                        for t in range(TT):
                            for q in range(4):
                                e = pe.transpose(out_banks[half * TT + t][:, q // 2, (q % 2) * P:(q % 2 + 1) * P],
                                                 memt[:, half * 4 + q, t * P:(t + 1) * P], ident[:, :])
                            e.then_inc(tr_done, 1)
                    pe.wait_ge(sum_ready, su[0] + 1)
                    for t in range(TT):
                        for b in range(UB):
                            e = pe.matmul(stat[:, t, 0:P], ssum[:, b, t * P:(t + 1) * P], ones[:, :], start=(b == 0), stop=(b == UB - 1))
                    e.then_inc(stat_ready, 1)


_INS = ["x", "mem", "norm_mix", "norm_xattn", "norm_mem", "norm_ffn", "norm_final",
        "a_w_in", "a_conv", "a_w_out",
        "b_w_qkv", "b_b_qkv", "b_sinks", "b_w_o", "b_b_o",
        "c_w_pw1", "c_b_pw1", "c_w_dw", "c_b_dw", "c_ln_g", "c_ln_b", "c_w_pw2", "c_b_pw2",
        "x_w_q", "x_w_kv", "x_w_o", "f_w_up", "f_conv", "f_w_down"]


def kernel(**inputs):
    import numpy as _np
    import concourse.bacc as _bacc
    from concourse import mybir as _mybir
    from concourse.bass_utils import run_bass_kernel_spmd as _run

    nc = _bacc.Bacc("TRN2", target_bir_lowering=False, num_devices=1)
    arrays, aps = {}, {}
    for name in _INS:
        v = _np.ascontiguousarray(inputs[name])
        arrays[f"in_{name}"] = v
        aps[name] = nc.dram_tensor(f"in_{name}", v.shape, _mybir.dt.from_np(v.dtype), kind="ExternalInput").ap()
    out = nc.dram_tensor("out", (1, T, D), F32, kind="ExternalOutput").ap()
    build(nc, aps, out)
    r = _run(nc, [arrays], core_ids=[0])
    return r.results[0]["out"]
```
